# Optimizing a Trainium2 kernel written in Bass

```python
import jax, jax.numpy as jnp
from jax import lax
import numpy as np

D_MODEL = 1024
BATCH = 1
SEQ = 256
DEPTH = 2

ATTN_HEADS = 16
HEAD_DIM = 64
ATTN_WIDTH = ATTN_HEADS * HEAD_DIM
IDX_HEADS = 8
IDX_DIM = 64
IDX_SCALE = (IDX_HEADS ** -0.5) * (IDX_DIM ** -0.5)
TOPK_MAX = 256
Q_BLOCK = 128
ROPE_THETA = 10000.0
D_INNER = 2 * D_MODEL
SSM_HEAD_DIM = 64
SSM_HEADS = D_INNER // SSM_HEAD_DIM
SSM_GROUPS = 4
HEADS_PER_GROUP = SSM_HEADS // SSM_GROUPS
D_STATE = 128
SSM_CONV = 4
SSM_CHUNK = 256
XBC_WIDTH = D_INNER + 2 * SSM_GROUPS * D_STATE
D_FF = 2816
FFN_CONV = 3
EPS = 1e-6
SPLITS = (ATTN_WIDTH, ATTN_WIDTH, ATTN_WIDTH, IDX_HEADS * IDX_DIM, IDX_DIM, IDX_HEADS,
          D_INNER, XBC_WIDTH, SSM_HEADS, D_MODEL, D_MODEL)
IN_WIDTH = sum(SPLITS)
SPLIT_POINTS = tuple(int(v) for v in np.cumsum(SPLITS)[:-1])


def rms_norm(x, g):
    xf = x.astype(jnp.float32)
    y = xf * lax.rsqrt(jnp.mean(xf * xf, axis=-1, keepdims=True) + EPS)
    return (y * g.astype(jnp.float32)).astype(x.dtype)

def rope_tables(positions, dim):
    inv = 1.0 / (ROPE_THETA ** (jnp.arange(0, dim, 2, dtype=jnp.float32) / dim))
    ang = positions.astype(jnp.float32)[..., None] * inv
    return jnp.cos(ang), jnp.sin(ang)

def apply_rope(x, cos, sin):
    xf = x.astype(jnp.float32)
    x1, x2 = jnp.split(xf, 2, axis=-1)
    c = cos[:, :, None, :]
    s = sin[:, :, None, :]
    return jnp.concatenate([x1 * c - x2 * s, x2 * c + x1 * s], axis=-1).astype(x.dtype)

def causal_dwconv(x, w, b):
    width = w.shape[0]
    y = lax.conv_general_dilated(
        x, w[:, None, :].astype(x.dtype), window_strides=(1,), padding=[(width - 1, 0)],
        dimension_numbers=("NWC", "WIO", "NWC"), feature_group_count=x.shape[-1])
    return y + b.astype(x.dtype)

def dsa_attention(q, k, v, iq, ik, iw, n_keep):
    bsz, seq = q.shape[:2]
    n_blocks = seq // Q_BLOCK
    kpos = jnp.arange(seq)
    scale = HEAD_DIM ** -0.5

    def block(i):
        start = i * Q_BLOCK
        qb = lax.dynamic_slice_in_dim(q, start, Q_BLOCK, axis=1)
        iqb = lax.dynamic_slice_in_dim(iq, start, Q_BLOCK, axis=1)
        iwb = lax.dynamic_slice_in_dim(iw, start, Q_BLOCK, axis=1)
        qpos = start + jnp.arange(Q_BLOCK)
        causal = kpos[None, :] <= qpos[:, None]
        logits = jnp.einsum("bqhd,bsd->bqhs", iqb, ik)
        score = jnp.einsum("bqh,bqhs->bqs", iwb, jax.nn.relu(logits)).astype(jnp.float32) * IDX_SCALE
        score = jnp.where(causal[None], score, -jnp.inf)
        _, sel = lax.top_k(score, n_keep)
        kg = jax.vmap(lambda kb, ib: kb[ib])(k, sel)
        vg = jax.vmap(lambda vb, ib: vb[ib])(v, sel)
        s = jnp.einsum("bqhd,bqkhd->bhqk", qb, kg).astype(jnp.float32) * scale
        valid = sel <= qpos[None, :, None]
        s = jnp.where(valid[:, None], s, -jnp.inf)
        p = jax.nn.softmax(s, axis=-1).astype(v.dtype)
        return jnp.einsum("bhqk,bqkhd->bqhd", p, vg)

    out = lax.map(block, jnp.arange(n_blocks))
    return out.transpose(1, 0, 2, 3, 4).reshape(bsz, seq, ATTN_WIDTH)

def segsum(a):
    t = a.shape[-1]
    cs = jnp.cumsum(a, axis=-1)
    seg = cs[..., :, None] - cs[..., None, :]
    mask = jnp.tril(jnp.ones((t, t), dtype=bool))
    return jnp.where(mask, seg, -jnp.inf)

def ssd_scan(xs, a, bm, cm):
    bsz, seq = xs.shape[:2]
    t = SSM_CHUNK
    pad = (-seq) % t
    if pad:
        padw = lambda z: jnp.pad(z, [(0, 0), (0, pad)] + [(0, 0)] * (z.ndim - 2))
        xs, a, bm, cm = padw(xs), padw(a), padw(bm), padw(cm)
    nc = (seq + pad) // t
    xs_c = xs.reshape(bsz, nc, t, SSM_GROUPS, HEADS_PER_GROUP, SSM_HEAD_DIM)
    bm_c = bm.reshape(bsz, nc, t, SSM_GROUPS, D_STATE)
    cm_c = cm.reshape(bsz, nc, t, SSM_GROUPS, D_STATE)
    a_c = a.reshape(bsz, nc, t, SSM_GROUPS, HEADS_PER_GROUP).transpose(0, 3, 4, 1, 2)
    a_cs = jnp.cumsum(a_c, axis=-1)
    decay = jnp.exp(segsum(a_c))
    cb = jnp.einsum("bclgn,bcsgn->bgcls", cm_c, bm_c)
    y_diag = jnp.einsum("bgcls,bgrcls,bcsgrp->bclgrp", cb, decay, xs_c)
    decay_states = jnp.exp(a_cs[..., -1:] - a_cs)
    states = jnp.einsum("bclgn,bgrcl,bclgrp->bcgrpn", bm_c, decay_states, xs_c)
    states = jnp.concatenate([jnp.zeros_like(states[:, :1]), states], axis=1)
    chunk_decay = jnp.exp(segsum(jnp.pad(a_cs[..., -1], ((0, 0), (0, 0), (0, 0), (1, 0)))))
    prev_states = jnp.einsum("bgrzc,bcgrpn->bzgrpn", chunk_decay, states)[:, :-1]
    y_off = jnp.einsum("bclgn,bcgrpn,bgrcl->bclgrp", cm_c, prev_states, jnp.exp(a_cs))
    y = (y_diag + y_off).reshape(bsz, nc * t, SSM_GROUPS, HEADS_PER_GROUP, SSM_HEAD_DIM)[:, :seq]
    return y.astype(xs.dtype)

def first_inputs(seed: int = 0) -> dict:
    key = jax.random.key(seed)
    ks = jax.random.split(key, 28)
    f32 = jnp.float32

    def nrm(k, shape, fan_in, gain=1.0):
        return jax.random.normal(k, shape, f32) * (gain * fan_in ** -0.5)

    def gain_vec(k, shape):
        return 1.0 + 0.1 * jax.random.normal(k, shape, f32)

    x = jax.random.normal(ks[0], (BATCH, SEQ, D_MODEL), f32)
    c = jax.random.normal(ks[1], (BATCH, D_MODEL), f32)
    start = jax.random.randint(ks[2], (BATCH, 1), 0, 4096, dtype=jnp.int32)
    positions = start + jnp.arange(SEQ, dtype=jnp.int32)[None, :]
    dt0 = jnp.exp(jax.random.uniform(ks[3], (DEPTH, SSM_HEADS), f32, np.log(1e-3), np.log(1e-1)))
    dt_bias = dt0 + jnp.log(-jnp.expm1(-dt0))
    a_log = jnp.log(jax.random.uniform(ks[4], (DEPTH, SSM_HEADS), f32, 1.0, 16.0))
    return {
        "x": x,
        "c": c,
        "positions": positions,
        "w_ada": nrm(ks[5], (DEPTH, D_MODEL, 6 * D_MODEL), D_MODEL, 0.5),
        "b_ada": 0.01 * jax.random.normal(ks[6], (DEPTH, 6 * D_MODEL), f32),
        "norm1_g": gain_vec(ks[7], (DEPTH, D_MODEL)),
        "w_in": nrm(ks[8], (DEPTH, D_MODEL, IN_WIDTH), D_MODEL),
        "q_norm_g": gain_vec(ks[9], (DEPTH, HEAD_DIM)),
        "k_norm_g": gain_vec(ks[10], (DEPTH, HEAD_DIM)),
        "ssm_conv_w": nrm(ks[11], (DEPTH, SSM_CONV, XBC_WIDTH), SSM_CONV),
        "ssm_conv_b": 0.01 * jax.random.normal(ks[12], (DEPTH, XBC_WIDTH), f32),
        "dt_bias": dt_bias,
        "a_log": a_log,
        "d_skip": gain_vec(ks[13], (DEPTH, SSM_HEADS)),
        "ssm_norm_g": gain_vec(ks[14], (DEPTH, D_INNER)),
        "w_attn_o": nrm(ks[15], (DEPTH, ATTN_WIDTH, D_MODEL), ATTN_WIDTH),
        "w_ssm_o": nrm(ks[16], (DEPTH, D_INNER, D_MODEL), D_INNER),
        "w_out": nrm(ks[17], (DEPTH, D_MODEL, D_MODEL), D_MODEL),
        "norm2_g": gain_vec(ks[18], (DEPTH, D_MODEL)),
        "w_up": nrm(ks[19], (DEPTH, D_MODEL, 2 * D_FF), D_MODEL),
        "ffn_conv_w": nrm(ks[20], (DEPTH, FFN_CONV, 2 * D_FF), FFN_CONV),
        "ffn_conv_b": 0.01 * jax.random.normal(ks[21], (DEPTH, 2 * D_FF), f32),
        "w_down": nrm(ks[22], (DEPTH, D_FF, D_MODEL), D_FF),
    }

def first_block(x, c, positions, w_ada, b_ada, norm1_g, w_in, q_norm_g, k_norm_g, ssm_conv_w, ssm_conv_b,
              dt_bias, a_log, d_skip, ssm_norm_g, w_attn_o, w_ssm_o, w_out, norm2_g, w_up, ffn_conv_w,
              ffn_conv_b, w_down):
    bsz, seq, _ = x.shape
    n_keep = min(TOPK_MAX, seq // 4)
    cos, sin = rope_tables(positions, HEAD_DIM)
    c_act = jax.nn.silu(c)

    for l in range(DEPTH):
        mod = c_act @ w_ada[l] + b_ada[l]
        sh1, sc1, g1, sh2, sc2, g2 = [m[:, None, :] for m in jnp.split(mod, 6, axis=-1)]

        h = rms_norm(x, norm1_g[l]) * (1.0 + sc1) + sh1
        proj = h @ w_in[l]
        q, k, v, iq, ik, iw, z, xbc, dt_raw, ga, gm = jnp.split(proj, SPLIT_POINTS, axis=-1)

        q = apply_rope(rms_norm(q.reshape(bsz, seq, ATTN_HEADS, HEAD_DIM), q_norm_g[l]), cos, sin)
        k = apply_rope(rms_norm(k.reshape(bsz, seq, ATTN_HEADS, HEAD_DIM), k_norm_g[l]), cos, sin)
        v = v.reshape(bsz, seq, ATTN_HEADS, HEAD_DIM)
        iq = apply_rope(iq.reshape(bsz, seq, IDX_HEADS, IDX_DIM), cos, sin)
        ik = apply_rope(ik[:, :, None, :], cos, sin)[:, :, 0, :]
        o_attn = dsa_attention(q, k, v, iq, ik, iw, n_keep) @ w_attn_o[l]

        xbc = jax.nn.silu(causal_dwconv(xbc, ssm_conv_w[l], ssm_conv_b[l]))
        xs, bm, cm = jnp.split(xbc, [D_INNER, D_INNER + SSM_GROUPS * D_STATE], axis=-1)
        xs = xs.reshape(bsz, seq, SSM_GROUPS, HEADS_PER_GROUP, SSM_HEAD_DIM)
        bm = bm.reshape(bsz, seq, SSM_GROUPS, D_STATE)
        cm = cm.reshape(bsz, seq, SSM_GROUPS, D_STATE)
        dt = jax.nn.softplus(dt_raw.astype(jnp.float32) + dt_bias[l].astype(jnp.float32))
        a_cont = -jnp.exp(a_log[l].astype(jnp.float32))
        a_dt = (dt * a_cont).reshape(bsz, seq, SSM_GROUPS, HEADS_PER_GROUP)
        dt_g = dt.reshape(bsz, seq, SSM_GROUPS, HEADS_PER_GROUP, 1).astype(xs.dtype)
        y = ssd_scan(xs * dt_g, a_dt, bm, cm)
        y = y + xs * d_skip[l].reshape(SSM_GROUPS, HEADS_PER_GROUP, 1)
        y = y.reshape(bsz, seq, D_INNER) * jax.nn.silu(z)
        y = rms_norm(y.reshape(bsz, seq, SSM_GROUPS, D_INNER // SSM_GROUPS),
                     ssm_norm_g[l].reshape(SSM_GROUPS, D_INNER // SSM_GROUPS)).reshape(bsz, seq, D_INNER)
        o_ssm = y @ w_ssm_o[l]

        mixed = (jax.nn.sigmoid(ga) * o_attn + jax.nn.sigmoid(gm) * o_ssm) @ w_out[l]
        x = x + g1 * mixed

        h = rms_norm(x, norm2_g[l]) * (1.0 + sc2) + sh2
        u = causal_dwconv(h @ w_up[l], ffn_conv_w[l], ffn_conv_b[l])
        val, gate = jnp.split(u, 2, axis=-1)
        x = x + g2 * ((jax.nn.silu(gate) * val) @ w_down[l])

    return x


DEPTH_2 = 1

N_HEADS = D_MODEL // HEAD_DIM
N_MOBA = N_HEADS // 4
N_FOX = (N_HEADS - N_MOBA) // 2
N_DIL = N_HEADS - N_MOBA - N_FOX
N_ALIBI = N_MOBA + N_DIL
MOBA_BLOCK = 256
MOBA_TOPK = 3
MOBA_QCHUNK = 32
FOX_QBLOCK = 128
DIL_PAIRS = ((128, 1), (512, 4), (2048, 16))
DIL_BLOCK = 128
D_FF_2 = 4 * D_MODEL
QKV_COLS = 3 * D_MODEL
FOX_GATE_COLS = N_FOX * HEAD_DIM
N_IN_COLS = QKV_COLS + N_FOX + FOX_GATE_COLS
W_MOBA = N_MOBA * HEAD_DIM
W_FOX = N_FOX * HEAD_DIM
ATTN_SCALE = HEAD_DIM ** -0.5
NEG_INF = -1e30


def rms_norm_2(x, gain):
    xf = x.astype(jnp.float32)
    y = xf * lax.rsqrt(jnp.mean(xf * xf, axis=-1, keepdims=True) + EPS)
    return (y * gain.astype(jnp.float32)).astype(x.dtype)

def alibi_slopes():
    return jnp.exp2(-8.0 * jnp.arange(1, N_ALIBI + 1, dtype=jnp.float32) / N_ALIBI)

def moba_attention(q, k, v, slopes):
    b, h, s, dh = q.shape
    n_blk = -(-s // MOBA_BLOCK)
    s_pad = n_blk * MOBA_BLOCK
    pad = ((0, 0), (0, 0), (0, s_pad - s), (0, 0))
    q, k, v = jnp.pad(q, pad), jnp.pad(k, pad), jnp.pad(v, pad)
    k_blocks = k.reshape(b, h, n_blk, MOBA_BLOCK, dh)
    v_blocks = v.reshape(b, h, n_blk, MOBA_BLOCK, dh)
    k_mean = jnp.mean(k_blocks.astype(jnp.float32), axis=3)
    gate = jnp.einsum('bhsd,bhnd->bhsn', q.astype(jnp.float32), k_mean)
    q_blk = jnp.arange(s_pad) // MOBA_BLOCK
    past = jnp.arange(n_blk)[None, :] < q_blk[:, None]
    gate = jnp.where(past, gate, NEG_INF)
    top_k = min(MOBA_TOPK, n_blk)
    _, sel_idx = lax.top_k(gate, top_k)
    sel_ok = sel_idx < q_blk[:, None]
    gather = jax.vmap(jax.vmap(lambda blocks, idx: blocks[idx]))
    offs = jnp.arange(MOBA_BLOCK)

    def chunk(c):
        start = c * MOBA_QCHUNK
        qc = lax.dynamic_slice_in_dim(q, start, MOBA_QCHUNK, axis=2)
        idx = lax.dynamic_slice_in_dim(sel_idx, start, MOBA_QCHUNK, axis=2)
        ok = lax.dynamic_slice_in_dim(sel_ok, start, MOBA_QCHUNK, axis=2)
        q_pos = start + jnp.arange(MOBA_QCHUNK)
        k_sel = gather(k_blocks, idx)
        v_sel = gather(v_blocks, idx)
        d_sel = (q_pos[:, None, None] - (idx[..., None] * MOBA_BLOCK + offs)).astype(jnp.float32)
        l_sel = (jnp.einsum('bhqd,bhqnkd->bhqnk', qc, k_sel).astype(jnp.float32) * ATTN_SCALE
                 - slopes[:, None, None, None] * d_sel)
        l_sel = jnp.where(ok[..., None], l_sel, NEG_INF).reshape(b, h, MOBA_QCHUNK, top_k * MOBA_BLOCK)
        own_start = (start // MOBA_BLOCK) * MOBA_BLOCK
        k_own = lax.dynamic_slice_in_dim(k, own_start, MOBA_BLOCK, axis=2)
        v_own = lax.dynamic_slice_in_dim(v, own_start, MOBA_BLOCK, axis=2)
        d_own = q_pos[:, None] - (own_start + offs)[None, :]
        l_own = (jnp.einsum('bhqd,bhkd->bhqk', qc, k_own).astype(jnp.float32) * ATTN_SCALE
                 - slopes[:, None, None] * d_own.astype(jnp.float32))
        l_own = jnp.where(d_own >= 0, l_own, NEG_INF)
        p = jax.nn.softmax(jnp.concatenate([l_sel, l_own], axis=-1), axis=-1).astype(v.dtype)
        p_sel = p[..., :top_k * MOBA_BLOCK].reshape(b, h, MOBA_QCHUNK, top_k, MOBA_BLOCK)
        return (jnp.einsum('bhqnk,bhqnkd->bhqd', p_sel, v_sel)
                + jnp.einsum('bhqk,bhkd->bhqd', p[..., top_k * MOBA_BLOCK:], v_own))

    out = lax.map(chunk, jnp.arange(s_pad // MOBA_QCHUNK))
    return out.transpose(1, 2, 0, 3, 4).reshape(b, h, s_pad, dh)[:, :, :s]

def forgetting_attention(q, k, v, f_logit):
    b, h, s, dh = q.shape
    cum = jnp.cumsum(jax.nn.log_sigmoid(f_logit.astype(jnp.float32)), axis=1).transpose(0, 2, 1)
    k_pos = jnp.arange(s)

    def block(i):
        start = i * FOX_QBLOCK
        qb = lax.dynamic_slice_in_dim(q, start, FOX_QBLOCK, axis=2)
        cb = lax.dynamic_slice_in_dim(cum, start, FOX_QBLOCK, axis=2)
        q_pos = start + jnp.arange(FOX_QBLOCK)
        logits = (jnp.einsum('bhqd,bhkd->bhqk', qb, k).astype(jnp.float32) * ATTN_SCALE
                  + cb[..., None] - cum[:, :, None, :])
        logits = jnp.where(k_pos[None, :] <= q_pos[:, None], logits, NEG_INF)
        p = jax.nn.softmax(logits, axis=-1).astype(v.dtype)
        return jnp.einsum('bhqk,bhkd->bhqd', p, v)

    out = lax.map(block, jnp.arange(s // FOX_QBLOCK))
    return out.transpose(1, 2, 0, 3, 4).reshape(b, h, s, dh)

def dilated_branch(q, k, v, slopes, window, dilation):
    b, h, s, dh = q.shape
    steps = window // dilation
    sub_len = s // dilation
    n_blk = -(-sub_len // DIL_BLOCK)
    sub_pad = n_blk * DIL_BLOCK

    def to_sub(t):
        t = t.reshape(b, h, sub_len, dilation, dh).transpose(0, 1, 3, 2, 4)
        t = jnp.pad(t, ((0, 0), (0, 0), (0, 0), (0, sub_pad - sub_len), (0, 0)))
        return t.reshape(b, h, dilation, n_blk, DIL_BLOCK, dh)

    def band(t):
        prev = jnp.concatenate([jnp.zeros_like(t[:, :, :, :1]), t[:, :, :, :-1]], axis=3)
        return jnp.concatenate([prev, t], axis=4)

    qs = to_sub(q)
    kb, vb = band(to_sub(k)), band(to_sub(v))
    blk = jnp.arange(n_blk)[:, None]
    i_q = blk * DIL_BLOCK + jnp.arange(DIL_BLOCK)[None, :]
    i_k = (blk - 1) * DIL_BLOCK + jnp.arange(2 * DIL_BLOCK)[None, :]
    off = i_q[:, :, None] - i_k[:, None, :]
    allowed = (off >= 0) & (off <= steps) & (i_k[:, None, :] >= 0) & (i_k[:, None, :] < sub_len)
    dist = (off * dilation).astype(jnp.float32)
    logits = (jnp.einsum('bhrnqd,bhrnkd->bhrnqk', qs, kb).astype(jnp.float32) * ATTN_SCALE
              - slopes[:, None, None, None, None] * dist)
    logits = jnp.where(allowed, logits, NEG_INF)
    lse = jax.nn.logsumexp(logits, axis=-1)
    p = jnp.exp(logits - lse[..., None]).astype(v.dtype)
    o = jnp.einsum('bhrnqk,bhrnkd->bhrnqd', p, vb)
    o = o.reshape(b, h, dilation, sub_pad, dh)[:, :, :, :sub_len].transpose(0, 1, 3, 2, 4).reshape(b, h, s, dh)
    lse = lse.reshape(b, h, dilation, sub_pad)[..., :sub_len].transpose(0, 1, 3, 2).reshape(b, h, s)
    return o, lse

def dilated_attention(q, k, v, slopes):
    outs, lses = [], []
    for window, dilation in DIL_PAIRS:
        o, lse = dilated_branch(q, k, v, slopes, window, dilation)
        outs.append(o)
        lses.append(lse)
    w = jax.nn.softmax(jnp.stack(lses, axis=0), axis=0)
    o = jnp.sum(w[..., None] * jnp.stack(outs, axis=0).astype(jnp.float32), axis=0)
    return o.astype(q.dtype)

def to_bsd(o):
    b, h, s, dh = o.shape
    return o.transpose(0, 2, 1, 3).reshape(b, s, h * dh)

def mixer_sublayer(x, norm_g, w_in, b_f, q_gain, k_gain, out_gain, w_out):
    b, s, _ = x.shape
    hn = rms_norm_2(x, norm_g)
    proj = hn @ w_in
    q = proj[..., :D_MODEL].reshape(b, s, N_HEADS, HEAD_DIM)
    k = proj[..., D_MODEL:2 * D_MODEL].reshape(b, s, N_HEADS, HEAD_DIM)
    v = proj[..., 2 * D_MODEL:QKV_COLS].reshape(b, s, N_HEADS, HEAD_DIM)
    f_logit = proj[..., QKV_COLS:QKV_COLS + N_FOX] + b_f
    g_fox = proj[..., QKV_COLS + N_FOX:]
    q = rms_norm_2(q, q_gain).transpose(0, 2, 1, 3)
    k = rms_norm_2(k, k_gain).transpose(0, 2, 1, 3)
    v = v.transpose(0, 2, 1, 3)
    slopes = alibi_slopes()
    a0, a1 = N_MOBA, N_MOBA + N_FOX
    o_moba = moba_attention(q[:, :a0], k[:, :a0], v[:, :a0], slopes[N_DIL:])
    o_fox = forgetting_attention(q[:, a0:a1], k[:, a0:a1], v[:, a0:a1], f_logit)
    o_dil = dilated_attention(q[:, a1:], k[:, a1:], v[:, a1:], slopes[:N_DIL])
    y_moba = rms_norm_2(to_bsd(o_moba), out_gain[:W_MOBA])
    y_fox = rms_norm_2(to_bsd(o_fox), out_gain[W_MOBA:W_MOBA + W_FOX]) * jax.nn.sigmoid(g_fox)
    y_dil = rms_norm_2(to_bsd(o_dil), out_gain[W_MOBA + W_FOX:])
    y = jnp.concatenate([y_moba, y_fox, y_dil], axis=-1) @ w_out
    return x + y

def mlp_sublayer(x, norm_g, w_up, w_down):
    hn = rms_norm_2(x, norm_g)
    return x + jnp.square(jax.nn.relu(hn @ w_up)) @ w_down

def second_inputs(seed: int = 0) -> dict:
    key = jax.random.key(seed)
    ks = jax.random.split(key, 11)
    f32 = jnp.float32
    return {
        "x": jax.random.normal(ks[0], (BATCH, SEQ, D_MODEL), f32),
        "attn_norm": 1.0 + 0.02 * jax.random.normal(ks[1], (DEPTH_2, D_MODEL), f32),
        "w_in": jax.random.normal(ks[2], (DEPTH_2, D_MODEL, N_IN_COLS), f32) * D_MODEL ** -0.5,
        "b_forget": 2.0 + 0.5 * jax.random.normal(ks[3], (DEPTH_2, N_FOX), f32),
        "q_gain": 1.0 + 0.02 * jax.random.normal(ks[4], (DEPTH_2, N_HEADS, HEAD_DIM), f32),
        "k_gain": 1.0 + 0.02 * jax.random.normal(ks[5], (DEPTH_2, N_HEADS, HEAD_DIM), f32),
        "out_gain": 1.0 + 0.02 * jax.random.normal(ks[6], (DEPTH_2, D_MODEL), f32),
        "w_out": jax.random.normal(ks[7], (DEPTH_2, D_MODEL, D_MODEL), f32) * D_MODEL ** -0.5,
        "mlp_norm": 1.0 + 0.02 * jax.random.normal(ks[8], (DEPTH_2, D_MODEL), f32),
        "w_up": jax.random.normal(ks[9], (DEPTH_2, D_MODEL, D_FF_2), f32) * D_MODEL ** -0.5,
        "w_down": jax.random.normal(ks[10], (DEPTH_2, D_FF_2, D_MODEL), f32) * D_FF_2 ** -0.5,
    }

def second_block(x, attn_norm, w_in, b_forget, q_gain, k_gain, out_gain, w_out, mlp_norm, w_up, w_down):
    for l in range(DEPTH_2):
        x = mixer_sublayer(x, attn_norm[l], w_in[l], b_forget[l], q_gain[l], k_gain[l],
                           out_gain[l], w_out[l])
        x = mlp_sublayer(x, mlp_norm[l], w_up[l], w_down[l])
    return x


def setup_inputs(seed=0):
    out = dict(first_inputs(seed))
    for name, value in second_inputs(seed + 1).items():
        if name != "x":
            out[name + "_2"] = value
    return out


def reference(
    x, c, positions, w_ada, b_ada, norm1_g, w_in, q_norm_g, k_norm_g, ssm_conv_w, ssm_conv_b,
    dt_bias, a_log, d_skip, ssm_norm_g, w_attn_o, w_ssm_o, w_out, norm2_g, w_up, ffn_conv_w,
    ffn_conv_b, w_down, attn_norm_2, w_in_2, b_forget_2, q_gain_2, k_gain_2, out_gain_2,
    w_out_2, mlp_norm_2, w_up_2, w_down_2,
):
    x = first_block(
        x, c, positions, w_ada, b_ada, norm1_g, w_in, q_norm_g, k_norm_g, ssm_conv_w,
        ssm_conv_b, dt_bias, a_log, d_skip, ssm_norm_g, w_attn_o, w_ssm_o, w_out, norm2_g, w_up,
        ffn_conv_w, ffn_conv_b, w_down,
    )
    return second_block(
        x, attn_norm_2, w_in_2, b_forget_2, q_gain_2, k_gain_2, out_gain_2, w_out_2, mlp_norm_2,
        w_up_2, w_down_2,
    )


_drawn_inputs = setup_inputs


def setup_inputs(seed=0):
    import zlib

    import numpy as np

    out = dict(_drawn_inputs(seed))
    spreads = {}
    factors = {'q_norm_g': 7.449,
     'k_norm_g': 7.283,
     'ssm_conv_b': 8.0,
     'd_skip': 3.242,
     'ffn_conv_b': 8.0,
     'attn_norm_2': 2.978,
     'q_gain_2': 6.313,
     'k_gain_2': 6.254,
     'out_gain_2': 4.468,
     'mlp_norm_2': 3.542}
    for name, (base, spread) in spreads.items():
        noise = np.random.default_rng([zlib.crc32(name.encode()), seed]).standard_normal(out[name].shape)
        drawn = base * np.exp(spread * noise) if base else spread * noise
        out[name] = __import__('jax').numpy.asarray(drawn.astype(out[name].dtype))
    for name, factor in factors.items():
        out[name] = (out[name] * factor).astype(out[name].dtype)
    return out
```

```python
import math
from contextlib import ExitStack

import numpy as np
import concourse.bass as bass
from concourse import mybir

ds = bass.ds

P = 128
SEQ, D, DEPTH = 256, 1024, 2
TT = SEQ // P
KT = D // P
HEADS, HD = 16, 64
IDX_HEADS = 8
IDX_SCALE = (IDX_HEADS ** -0.5) * (HD ** -0.5)
KEEP = min(256, SEQ // 4)
TOP8 = KEEP // 8
D_INNER = 2 * D
SSM_HEADS, SSM_GROUPS, D_STATE = D_INNER // HD, 4, 128
XBC_TILES = (D_INNER + 2 * SSM_GROUPS * D_STATE) // P
SSM_CONV, FFN_CONV = 4, 3
D_FF, D_FF2 = 2816, 4096
FT, FT2 = D_FF // P, D_FF2 // P
N_MOBA, N_FOX, N_DIL = 4, 6, 6
G_COLS = N_FOX + N_FOX * HD
EPS = 1e-6
SCALE = HD ** -0.5
NEG = -1e30
PICKED = -3e38
CW = 3 * P

U_IDX, U_Q, U_KV, U_Z, U_XBC = 0, 4, 8, 16, 24
U_GA, U_GM, U_AO, U_SO, U_OUT, U_UP, U_DN = 36, 40, 44, 48, 56, 60, 82
DN_CHUNKS, DN2_CHUNKS = 6, 8
NCH = 2 * U_DN + 4 * DN_CHUNKS
NG = U_DN + 4
V_G, V_OUT, V_UP, V_DN = 12, 14, 18, 34
NCH2 = 2 * V_DN + 4 * DN2_CHUNKS
RING = 4
CHUNK = 4 * 256


def chunk_words(l, c):
    if l < DEPTH:
        if c // 2 == 2:
            return 4 * 72
        if c // 2 == 3:
            return 4 * 32
        if c >= 2 * U_DN and (c - 2 * U_DN) % DN_CHUNKS == DN_CHUNKS - 1:
            return 2 * 256
    elif c // 2 == V_G + 1:
        return 4 * (G_COLS - 256)
    return CHUNK


def chunk_count(l):
    return NCH if l < DEPTH else NCH2


N_CHUNKS = DEPTH * NCH + NCH2
OFFSETS = [0]
for _g in range(N_CHUNKS):
    _l = min(_g // NCH, DEPTH)
    OFFSETS.append(OFFSETS[-1] + P * chunk_words(_l, _g - _l * NCH))

PRM_PARTS = [("norm1", KT), ("norm2", KT), ("ssmn", 16), ("convb", XBC_TILES), ("convw", 4 * XBC_TILES),
             ("ffnb", 2 * FT), ("ffnw", 3 * 2 * FT), ("skip", 16), ("dtb", 32), ("alog", 32), ("qg", HD), ("kg", HD)]
PRM = {}
_at = 0
for _n, _w in PRM_PARTS:
    PRM[_n] = (_at, _at + _w)
    _at += _w
PRM_W = _at
CONST_PARTS = [("ident", P), ("causal", CW), ("maskT", P), ("inv", HD // 2)]
CST = {}
_at = 0
for _n, _w in CONST_PARTS:
    CST[_n] = (_at, _at + _w)
    _at += _w
CST_W = _at
PRM2_W = 2 * KT + N_FOX


class Banks:

    def __init__(self, new_bank, new_sem, name, per_layer):
        self.bank = [new_bank(f"{name}_bank{b}") for b in range(2)]
        self.full = [new_sem(f"{name}_full{b}") for b in range(2)]
        self.read = [new_sem(f"{name}_read{b}") for b in range(2)]
        self.per_layer = per_layer

    def use(self, l, i):
        b = i % 2
        return b, l * ((self.per_layer + 1 - b) // 2) + i // 2


def build(nc, x_t, c_col, pos, consts, alibi, params, b_ada, params2, rows2, w_ada, stream, out):
    f32, f32r, bf16, i32 = mybir.dt.float32, mybir.dt.float32r, mybir.dt.bfloat16, mybir.dt.int32
    ALU, ACT, AX = mybir.AluOpType, mybir.ActivationFunctionType, mybir.AxisListType
    ctx = ExitStack()
    with ctx:
        def sb(name, shape, dt=f32):
            return ctx.enter_context(nc.sbuf_tensor(name, shape, dt))

        def sem(name):
            return ctx.enter_context(nc.semaphore(name))

        w_raw = sb("w_raw", [P, RING, CHUNK])
        w_hi = sb("w_hi", [P, RING, CHUNK], f32r)
        w_lo = sb("w_lo", [P, RING, CHUNK], f32r)
        XT = sb("residual", [P, KT, SEQ])
        ada_w = sb("ada_w", [P, 2, KT * P])
        ada_acc = sb("ada_acc", [P, KT * P])
        cst = sb("consts_sb", [P, CST_W])
        prm = sb("params_sb", [P, PRM_W])
        prm2 = sb("params2_sb", [P, PRM2_W])
        bada = sb("b_ada_sb", [P, DEPTH * 48])
        mod = sb("mod", [P, DEPTH, 48])
        gain = sb("gain", [P, KT])
        ident_b = sb("ident_b", [P, P], bf16)
        maskT_b = sb("maskT_b", [P, P], bf16)
        ones = sb("ones", [P, SEQ])
        eps = sb("eps", [P, 1])
        c_act = sb("c_act", [P, KT])
        pos_i = sb("pos_i", [P, TT], i32)
        pos_f = sb("pos_f", [P, TT])
        sc_tab = sb("sin_cos", [P, 2, TT, 32])
        rt = sb("rope_tables", [P, 4, TT, 32])
        rs = sb("rstd_row", [P, 2, SEQ])
        probs = sb("probs", [P, 2, CW])
        probsT = sb("probsT", [P, 2, CW])
        keep_bias = sb("keep_bias", [P, CW])
        work = sb("work", [P, 4, 512])
        small = sb("small", [P, 256])
        root = sb("head_root", [P, 3, 32])
        neg_max = sb("neg_max", [P, HEADS, TT])
        row_max = sb("row_max", [P, HEADS, TT])
        row_sum = sb("row_sum", [P, HEADS, TT])
        row_inv = sb("row_inv", [P, HEADS, TT])
        iw = sb("idx_w", [P, TT, IDX_HEADS])
        dt_s = sb("dt", [P, TT, 32])
        neg_cs = sb("neg_cs", [P, TT, 32])
        a_row = sb("a_row", [32, SEQ])
        cs_row = sb("cs_row", [P, SEQ])
        conv = sb("conv", [P, 2, 512])

        def overlay(*sets):
            out, widest, top = [], 0, None
            for parts in sets:
                with ExitStack() as st:
                    row = []
                    total = 0
                    for name, shape, dt in parts:
                        row.append(st.enter_context(nc.sbuf_tensor(name, shape, dt)))
                        total += int(np.prod(shape[1:])) * 4
                    out.append(row)
                    if total > widest:
                        widest = total
            ctx.enter_context(nc.sbuf_tensor("region_" + sets[0][0][0], [P, widest // 4], f32))
            return out

        (HH, HL), (CB, xdt) = overlay(
            [("h_hi", [P, KT, SEQ], f32r), ("h_lo", [P, KT, SEQ], f32r)],
            [("c_dot_b", [P, SSM_GROUPS, CW], f32), ("x_dt", [P, TT, 1024], f32)])
        region = overlay(
            [("qkv", [P, 3, TT, D], f32),
             ("iq", [P, TT, 512], f32), ("iqT", [P, 4, SEQ], f32), ("ik", [P, TT, P], f32), ("ikT", [P, SEQ], f32),
             ("idx_relu", [P, 2, CW], f32), ("idx_score", [P, CW], f32), ("idx_left", [P, CW], f32),
             ("x_conv", [P, 16, SEQ], f32), ("bc_conv", [P, 8, SEQ], f32), ("z_gate", [P, 16, SEQ], f32)],
            [("sq", [P, KT, SEQ], f32), ("pad_a", [P, 16 * SEQ], f32), ("qT", [P, 8, SEQ], f32), ("kT", [P, 8, SEQ], f32)],
            [("gates", [P, 2, KT, SEQ], f32), ("pad_b", [P, 8 * SEQ], f32),
             ("oT_hi", [P, KT, SEQ], f32r), ("oT_lo", [P, KT, SEQ], f32r)],
            [("f_hi", [P, FT, SEQ], f32r), ("f_lo", [P, FT, SEQ], f32r)],
            [("f2_hi", [P, FT2, SEQ], f32r), ("f2_lo", [P, FT2, SEQ], f32r)],
            [("pad_c", [P, 40 * SEQ], f32), ("alibi_sb", [P, 10, CW], f32), ("fox_bias", [P, N_FOX, CW], f32),
             ("rows2_sb", [P, 3, D], f32), ("g2", [P, TT, G_COLS], f32)])
        (qkv, iq, iqT, ik, ikT, idx_relu, idx_score, idx_left, xs, bc, zg) = region[0]
        (sq, _, qT, kT), (gates, _, OTH, OTL), (FH, FL), (F2H, F2L), (_, alibi_sb, fox_bias, rows2_sb, g2) = region[1:]
        o_tok = qkv[:, 0]

        ident = cst[:, slice(*CST["ident"])]
        causal = cst[:, slice(*CST["causal"])]
        inv_freq = cst[:, slice(*CST["inv"])]

        def col(name, j, n=1):
            a = PRM[name][0] + j
            return prm[:, a:a + n]

        def bank(name):
            return ctx.enter_context(nc.psum_tensor(name, [P, 512], f32))

        gemm = [bank("gemm_bank0"), bank("gemm_bank1")]
        gemm_read = [sem("gemm_read0"), sem("gemm_read1")]
        S = Banks(bank, sem, "score", 60)
        T = Banks(bank, sem, "turn", 45)
        O = Banks(bank, sem, "outp", 22)
        mod_ps = S.bank[1][:, 384:384 + KT]
        T_IQ, T_A, T_CS, T_QK, T_AT, T_OT, T_XDT, T_SUM = 0, 3, 4, 5, 13, 29, None, None
        S_IDX, S_AT, S_CB, S_SSM = 0, 8, 24, 28
        O_N1, O_AT, O_Y, O_N2 = 0, 1, 5, 21

        def t_half(hf):
            return 33 + 6 * hf, 33 + 6 * hf + 4
        T2_A, T2_QK, T2_AT, T2_OT = 0, 1, 9, 25
        S2_FOX, S2_AT = 0, 6
        O2_N1, O2_AT, O2_N2 = 0, 1, 5

        raw_full = [sem(f"raw_full{s}") for s in range(RING)]
        hi_ready, lo_ready, chunk_done = sem("hi_ready"), sem("lo_ready"), sem("chunk_done")
        ada_full = [sem("ada_full0"), sem("ada_full1")]
        ada_used, ada_acc_ready, ada_sum, mod_ready = sem("ada_used"), sem("ada_acc_ready"), sem("ada_sum"), sem("mod_ready")
        in_full, prm_full, tab_full, out_full = sem("in_full"), sem("prm_full"), sem("tab_full"), sem("out_full")
        set_up, c_ready, sin_arg, sin_done = sem("set_up"), sem("c_ready"), sem("sin_arg"), sem("sin_done")
        sq_ready, x_root, h_scaled, h_hi_ready, h_ready = (
            sem("sq_ready"), sem("x_root"), sem("h_scaled"), sem("h_hi_ready"), sem("h_ready"))
        idx_rot, relu_used = sem("idx_rot"), sem("relu_used")
        qk_sum, qk_root, qk_rot = sem("qk_sum"), sem("qk_root"), sem("qk_rot")
        sp_in, sp_exp, a_ready, cs_ready, ncs_ready = sem("sp_in"), sem("sp_exp"), sem("a_ready"), sem("cs_ready"), sem("ncs_ready")
        conv_first, conv_act = sem("conv_first"), sem("conv_act")
        max_ready, exp_done, o_ready, o_full = sem("max_ready"), sem("exp_done"), sem("o_ready"), sem("o_full")
        oT_hi_ready, oT_ready = sem("oT_hi_ready"), sem("oT_ready")
        g_ready, y_done = sem("g_ready"), sem("y_done")
        y_gated, y_sq, y_root, y_scaled, y_hi, y_ready = (
            sem("y_gated"), sem("y_sq"), sem("y_root"), sem("y_scaled"), sem("y_hi"), sem("y_ready"))
        mix_ready, mix_hi, mix_low = sem("mix_ready"), sem("mix_hi"), sem("mix_low")
        up_first, up_silu, up_prod, up_hi, up_ready = (
            sem("up_first"), sem("up_silu"), sem("up_prod"), sem("up_hi"), sem("up_ready"))
        og_in, og_root, sig_done = sem("og_in"), sem("og_root"), sem("sig_done")

        block = ctx.enter_context(nc.Block())

        def first_chunk(l, u):
            return l * NCH + 2 * u

        def unit_end(l, u):
            return l * NCH + 2 * u + 2

        def gemm_use(l, o):
            return o % 2, l * (NG // 2) + o // 2

        def ada_group(l, g):
            return l * 6 + g

        @block.sync
        def _(sp):
            def load_chunk(g):
                l = min(g // NCH, DEPTH)
                n = chunk_words(l, g - l * NCH)
                if g >= RING:
                    sp.wait_ge(lo_ready, g - RING + 1)
                src = stream[OFFSETS[g]:OFFSETS[g + 1]].rearrange("(p n) -> p n", p=P)
                sp.dma_start(w_raw[:, g % RING, 0:n], src).then_inc(raw_full[g % RING], 16)

            def load_ada(grp, j):
                a = grp * KT + j
                if a >= 2:
                    sp.wait_ge(ada_used, a - 1)
                sp.dma_start(ada_w[:, a % 2, :], w_ada[a]).then_inc(ada_full[a % 2], 16)

            sp.dma_start(c_act[:], c_col).then_inc(in_full, 16)
            sp.dma_start(cst[:], consts).then_inc(in_full, 16)
            sp.dma_start(pos_i[:], pos).then_inc(in_full, 16)
            sp.dma_start(prm[:], params[0]).then_inc(prm_full, 16)
            sp.dma_start(bada[:], b_ada).then_inc(in_full, 16)
            sp.dma_start(prm2[:], params2).then_inc(in_full, 16)
            load_ada(0, 0)
            load_ada(0, 1)
            sp.dma_start(XT[:], x_t.rearrange("(k p) t -> p k t", p=P)).then_inc(in_full, 16)
            for a in range(2, 2 * KT):
                load_ada(a // KT, a % KT)
            for g in range(N_CHUNKS):
                l = min(g // NCH, DEPTH)
                c = g - l * NCH
                load_chunk(g)
                u = c // 2
                if l < DEPTH and c % 2 and U_GA <= u < U_SO + 4:
                    grp, j = (u - U_GA) // 4, (u - U_GA) % 4
                    load_ada(ada_group(l, 2 + grp), 2 * j)
                    load_ada(ada_group(l, 2 + grp), 2 * j + 1)
                if l + 1 < DEPTH and c % 2 and U_UP <= u < U_UP + 2 * KT:
                    j = u - U_UP
                    load_ada(ada_group(l + 1, j // KT), j % KT)
                if l < DEPTH and c == NCH - 1:
                    for b in range(2):
                        sp.wait_ge(gemm_read[b], gemm_use(l, U_DN - 2 + b)[1] + 1)
                    sp.wait_ge(up_first, (l + 1) * FT)
                    if l + 1 < DEPTH:
                        sp.dma_start(prm[:], params[l + 1]).then_inc(prm_full, 16)
                if l == DEPTH and c == 7:
                    sp.wait_ge(chunk_done, DEPTH * NCH)
                    sp.dma_start(alibi_sb[:], alibi).then_inc(tab_full, 16)
                    sp.dma_start(rows2_sb[:], rows2).then_inc(tab_full, 16)
            o3 = out.rearrange("(k p) t -> p k t", p=P)
            for j in range(4):
                b, k = gemm_use(DEPTH, V_DN + j)
                sp.wait_ge(gemm_read[b], k + 1)
                sp.dma_start(o3[:, 2 * j:2 * j + 2, :], XT[:, 2 * j:2 * j + 2, :]).then_inc(out_full, 16)
            sp.wait_ge(out_full, 64)

        @block.gpsimd
        def _(pool):
            for g in range(N_CHUNKS):
                l = min(g // NCH, DEPTH)
                n = chunk_words(l, g - l * NCH)
                s = g % RING
                pool.wait_ge(hi_ready, g + 1)
                if g >= RING:
                    pool.wait_ge(chunk_done, g - RING + 1)
                nc.gpsimd.tensor_tensor(w_lo[:, s, 0:n], w_raw[:, s, 0:n], w_hi[:, s, 0:n].bitcast(f32),
                                        ALU.subtract).then_inc(lo_ready, 1)

        @block.scalar
        def _(act):
            A = nc.scalar.activation

            def high(g):
                if g >= N_CHUNKS:
                    return
                l = min(g // NCH, DEPTH)
                n = chunk_words(l, g - l * NCH)
                s = g % RING
                act.wait_ge(raw_full[s], 16 * (g // RING + 1))
                if g >= RING:
                    act.wait_ge(chunk_done, g - RING + 1)
                A(w_hi[:, s, 0:n], w_raw[:, s, 0:n], ACT.Copy).then_inc(hi_ready, 1)

            def after_unit(l, u):
                for g in range(first_chunk(l, u), first_chunk(l, u) + 2):
                    high(g + RING)
                act.wait_ge(chunk_done, unit_end(l, u))

            def norm(l, which, bias, summed):
                for j in range(4):
                    if summed:
                        b, k = gemm_use(summed[0], summed[1] + j)
                        act.wait_ge(gemm_read[b], k + 1)
                    A(sq[:, 2 * j:2 * j + 2, :], XT[:, 2 * j:2 * j + 2, :], ACT.Square).then_inc(sq_ready, 1)
                n = 2 * l + which
                i = (O_N2 if which else O_N1) if l < DEPTH else (O2_N2 if which else O2_N1)
                b, k = O.use(l, i)
                act.wait_ge(O.read[b], k + 1)
                A(rs[:, 0, :], rs[:, 1, :], ACT.Sqrt).then_inc(x_root, 1)
                for kt in range(KT):
                    act.wait_ge(h_scaled, n * KT + kt + 1)
                    if bias is None:
                        A(HH[:, kt, :], sq[:, kt, :], ACT.Copy).then_inc(h_hi_ready, 1)
                    else:
                        A(HH[:, kt, :], sq[:, kt, :], ACT.Identity, bias=bias[:, kt:kt + 1]).then_inc(h_hi_ready, 1)

            def attention(l):
                s0, t0 = (S_AT, T_AT) if l < DEPTH else (S2_AT, T2_AT)
                for h in range(HEADS):
                    b = h % 2
                    act.wait_ge(max_ready, l * HEADS + h + 1)
                    A(probs[:, b, 0:P], probs[:, b, 0:P], ACT.Exp, scale=SCALE, bias=neg_max[:, h, 0:1],
                      accum_out=row_sum[:, h, 0:1])
                    A(probs[:, b, P:CW], probs[:, b, P:CW], ACT.Exp, scale=SCALE, bias=neg_max[:, h, 1:2],
                      accum_out=row_sum[:, h, 1:2]).then_inc(exp_done, 1)
                    if h >= 1 and (h - 1) % 2 == 0:
                        turn_evac(l, h - 1, t0)

            def turn_evac(l, h, t0):
                b, k = T.use(l, t0 + h)
                act.wait_ge(T.full[b], k + 1)
                A(probsT[:, h % 2, :], T.bank[b][:, 0:CW], ACT.Copy).then_inc(T.read[b], 1)

            def turn_qk(l, t0):
                for r in range(0, 8, 2):
                    b, k = T.use(l, t0 + r)
                    act.wait_ge(T.full[b], k + 1)
                    dst = qT if r < 4 else kT
                    j = 2 * (r % 4)
                    A(dst[:, j:j + 2, :], T.bank[b][:], ACT.Copy).then_inc(T.read[b], 1)

            def square_y(l, f):
                act.wait_ge(y_gated, l * 16 + f + 1)
                if f % 4 == 0 and f:
                    hf, gi = (f // 4 - 1) // 2, (f // 4 - 1) % 2
                    b, k = T.use(l, t_half(hf)[1] + gi)
                    act.wait_ge(T.full[b], k + 1)
                A(work[:, f % 4, SEQ:2 * SEQ], zg[:, f, :], ACT.Square).then_inc(y_sq, 1)

            def turn_o(l, t0):
                for r in range(4):
                    b, k = T.use(l, t0 + r)
                    act.wait_ge(T.full[b], k + 1)
                    A(OTH[:, 2 * r:2 * r + 2, :], T.bank[b][:], ACT.Copy).then_inc(oT_hi_ready, 1)

            act.wait_ge(in_full, 96)
            A(small[:, 0:KT], c_act[:], ACT.Tanh, scale=0.5).then_inc(c_ready, 1)
            act.wait_ge(sin_arg, 1)
            A(sc_tab[:], sc_tab[:], ACT.Sin).then_inc(sin_done, 1)
            for g in range(RING):
                high(g)

            for l in range(DEPTH):
                act.wait_ge(set_up, 1)
                act.wait_ge(mod_ready, ada_group(l, 1) + 1)
                norm(l, 0, mod[:, l, 0:KT], (l - 1, U_DN) if l else None)
                for u in range(U_IDX, U_Q):
                    after_unit(l, u)
                for u in range(U_Q, U_Z):
                    if u == U_KV:
                        for h in range(IDX_HEADS):
                            b, k = S.use(l, S_IDX + h)
                            act.wait_ge(S.full[b], k + 1)
                            if h >= 2:
                                act.wait_ge(relu_used, l * IDX_HEADS + h - 1)
                            A(idx_relu[:, h % 2, :], S.bank[b][:, 0:CW], ACT.Relu).then_inc(S.read[b], 1)
                    after_unit(l, u)
                    i, j = (u - U_Q) // 4, (u - U_Q) % 4
                    A(qkv[:, i, :, 256 * j:256 * j + 256], gemm[u % 2][:].rearrange("p (t n) -> p t n", t=TT),
                      ACT.Copy).then_inc(gemm_read[u % 2], 1)
                for u in range(U_Z, U_XBC):
                    if u == U_Z:
                        act.wait_ge(qk_sum, 2 * l + 1)
                        A(root[:, 0, :], small[:, 64:96], ACT.Sqrt).then_inc(qk_root, 1)
                    if u == U_Z + 2:
                        act.wait_ge(qk_sum, 2 * l + 2)
                        A(root[:, 1, :], small[:, 96:128], ACT.Sqrt).then_inc(qk_root, 1)
                    after_unit(l, u)
                    j = 2 * (u - U_Z)
                    A(zg[:, j:j + 2, :], gemm[u % 2][:], ACT.Silu).then_inc(gemm_read[u % 2], 1)
                act.wait_ge(sp_in, l + 1)
                A(small[:, 0:64], small[:, 0:64], ACT.Exp).then_inc(sp_exp, 1)
                A(small[:, 128:160], prm[:, slice(*PRM["alog"])], ACT.Exp).then_inc(sp_exp, 1)
                for u in range(U_XBC, U_GA):
                    after_unit(l, u)
                    v = u - U_XBC
                    if v >= 2:
                        act.wait_ge(conv_act, l * 12 + v - 1)
                    for j in range(2):
                        t = 2 * v + j
                        A(conv[:, v % 2, j * SEQ:(j + 1) * SEQ], gemm[u % 2][:, j * SEQ:(j + 1) * SEQ], ACT.Identity,
                          scale=col("convw", 3 * XBC_TILES + t), bias=col("convb", t)).then_inc(conv_first, 1)
                    b, k = gemm_use(l, u)
                    act.wait_ge(gemm_read[b], k + 1)
                    dst = xs[:, 2 * v:2 * v + 2, :] if v < 8 else bc[:, 2 * v - 16:2 * v - 14, :]
                    A(dst, conv[:, v % 2, :], ACT.Silu).then_inc(conv_act, 1)
                turn_qk(l, T_QK)
                attention(l)
                turn_o(l, T_OT)
                for u in range(U_GA, U_AO):
                    after_unit(l, u)
                    i, j = (u - U_GA) // 4, (u - U_GA) % 4
                    A(gates[:, i, 2 * j:2 * j + 2, :], gemm[u % 2][:], ACT.Sigmoid).then_inc(gemm_read[u % 2], 1)
                for u in range(U_AO, U_SO):
                    after_unit(l, u)
                for hf in range(2):
                    tx, ts = t_half(hf)
                    for h in range(16 * hf, 16 * hf + 16):
                        b, k = S.use(l, S_SSM + h)
                        act.wait_ge(S.full[b], k + 1)
                        n = l * 32 + h
                        if n >= 2:
                            act.wait_ge(g_ready, n - 1)
                        if h == 0:
                            act.wait_ge(ncs_ready, l + 1)
                        A(probs[:, b, 0:2 * P], S.bank[b][:, 0:2 * P], ACT.Exp, bias=neg_cs[:, 0, h:h + 1])
                        A(probs[:, b, 2 * P:CW], S.bank[b][:, 2 * P:CW], ACT.Exp, bias=neg_cs[:, 1, h:h + 1]
                          ).then_inc(S.read[b], 1)
                        if h % 2 and h > 16 * hf + 1:
                            square_y(l, h // 2 - 1)
                    square_y(l, 8 * hf + 7)
                    for gi in range(2):
                        b, k = T.use(l, ts + gi)
                        act.wait_ge(T.read[b], k + 1)
                        A(rs[:, gi, :], work[:, gi, 0:SEQ], ACT.Sqrt).then_inc(y_root, 1)
                    for f in range(8):
                        n = l * 16 + 8 * hf + f
                        act.wait_ge(y_scaled, n + 1)
                        if f == 0:
                            act.wait_ge(chunk_done, unit_end(l, U_SO - 1 + 4 * hf))
                        A(OTH[:, f, :], zg[:, 8 * hf + f, :], ACT.Copy).then_inc(y_hi, 1)
                    for u in range(U_SO + 4 * hf, U_SO + 4 * hf + 4):
                        after_unit(l, u)
                for j in range(4):
                    act.wait_ge(mix_ready, l * 4 + j + 1)
                    A(HH[:, 2 * j:2 * j + 2, :], gates[:, 0, 2 * j:2 * j + 2, :], ACT.Copy).then_inc(mix_hi, 1)
                for u in range(U_OUT, U_UP):
                    after_unit(l, u)
                norm(l, 1, mod[:, l, 24:32], (l, U_OUT))
                for u in range(U_UP, U_DN):
                    after_unit(l, u)
                    i = u - U_UP
                    n = l * FT + i
                    if n >= 2:
                        act.wait_ge(up_ready, n - 1)
                    for j in range(2):
                        t = j * FT + i
                        a = A(conv[:, i % 2, j * SEQ:(j + 1) * SEQ], gemm[u % 2][:, j * SEQ:(j + 1) * SEQ], ACT.Identity,
                              scale=col("ffnw", 2 * 2 * FT + t), bias=col("ffnb", t))
                    a.then_inc(up_first, 1)
                    b, k = gemm_use(l, u)
                    act.wait_ge(gemm_read[b], k + 1)
                    A(work[:, i % 2, 0:SEQ], conv[:, i % 2, SEQ:2 * SEQ], ACT.Silu).then_inc(up_silu, 1)
                    act.wait_ge(up_prod, n + 1)
                    A(FH[:, i, :], work[:, i % 2, 0:SEQ], ACT.Copy).then_inc(up_hi, 1)
                for g in range(l * NCH + 2 * U_DN, (l + 1) * NCH):
                    high(g + RING)

            l = DEPTH
            norm(l, 0, None, (l - 1, U_DN))
            for u in range(0, V_G + 2):
                after_unit(l, u)
                if u < V_G:
                    i, j = u // 4, u % 4
                    A(qkv[:, i, :, 256 * j:256 * j + 256], gemm[u % 2][:].rearrange("p (t n) -> p t n", t=TT),
                      ACT.Copy).then_inc(gemm_read[u % 2], 1)
                else:
                    a, n = (0, 256) if u == V_G else (256, G_COLS - 256)
                    A(g2[:, :, a:a + n], gemm[u % 2][:].rearrange("p (t n) -> p t n", t=TT)[:, :, 0:n],
                      ACT.Copy).then_inc(gemm_read[u % 2], 1)
                if u == 8 or u == 12:
                    i = u // 12
                    act.wait_ge(qk_sum, 2 * l + i + 1)
                    A(root[:, i, :], small[:, 64 + 32 * i:96 + 32 * i], ACT.Sqrt).then_inc(qk_root, 1)
            act.wait_ge(sp_in, l + 1)
            A(small[:, 0:2 * N_FOX], small[:, 0:2 * N_FOX], ACT.Exp).then_inc(sp_exp, 1)
            turn_qk(l, T2_QK)
            attention(l)
            A(g2[:, :, N_FOX:], g2[:, :, N_FOX:], ACT.Sigmoid).then_inc(sig_done, 1)
            act.wait_ge(og_in, 1)
            A(root[:, 2, 0:6], small[:, 0:6], ACT.Sqrt).then_inc(og_root, 1)
            turn_o(l, T2_OT)
            for u in range(V_OUT, V_UP):
                after_unit(l, u)
            norm(l, 1, None, (l, V_OUT))
            for u in range(V_UP, V_DN):
                after_unit(l, u)
                i = u - V_UP
                n = DEPTH * FT + i
                act.wait_ge(up_ready, n - 1)
                A(conv[:, i % 2, :], gemm[u % 2][:], ACT.Relu).then_inc(up_first, 1)
                b, k = gemm_use(l, u)
                act.wait_ge(gemm_read[b], k + 1)
                A(F2H[:, 2 * i:2 * i + 2, :], work[:, i % 2, :], ACT.Copy).then_inc(up_hi, 1)
            for g in range(l * NCH + 2 * V_DN, N_CHUNKS - RING):
                high(g + RING)

        @block.vector
        def _(dve):
            V = nc.vector

            def stt(out, in0, scalar, in1, op0, op1):
                return V.scalar_tensor_tensor(out=out, in0=in0, scalar=scalar, in1=in1, op0=op0, op1=op1)

            def ada(grp, j):
                a = grp * KT + j
                dve.wait_ge(ada_full[a % 2], 16 * (a // 2 + 1))
                w = ada_w[:, a % 2, :].rearrange("p (k n) -> p k n", k=KT)
                acc = ada_acc[:, j * P:(j + 1) * P]
                if j == 0 and grp:
                    dve.wait_ge(ada_sum, grp)
                ins = V.tensor_scalar(acc, w[:, 0, :], c_act[:, 0:1], None, ALU.mult)
                for k in range(1, KT):
                    dve.drain()
                    if k == KT - 1:
                        ins = stt(acc, w[:, k, :], c_act[:, k:k + 1], acc, ALU.mult, ALU.add)
                    else:
                        stt(acc, w[:, k, :], c_act[:, k:k + 1], acc, ALU.mult, ALU.add)
                ins.then_inc(ada_used, 1)

            def mods(grp):
                dve.wait_ge(ada_sum, grp + 1)
                l, g = grp // 6, grp % 6
                V.tensor_tensor(mod[:, l, 8 * g:8 * g + 8], mod_ps, bada[:, 48 * l + 8 * g:48 * l + 8 * g + 8],
                                ALU.add).then_inc(mod_ready, 1)

            def rsqrt(r, v, w):
                V.reciprocal(r, r)
                dve.drain()
                V.tensor_tensor(w, r, r, ALU.mult)
                dve.drain()
                V.tensor_tensor(w, w, v, ALU.mult)
                dve.drain()
                V.tensor_scalar(w, w, -0.5, 1.5, ALU.mult, ALU.add)
                dve.drain()
                ins = V.tensor_tensor(r, r, w, ALU.mult)
                dve.drain()
                return ins

            def norm(l, which, g_col, scale_col, shift):
                n = 2 * l + which
                if scale_col is None:
                    V.tensor_copy(gain[:], g_col)
                else:
                    stt(gain[:], scale_col, 1.0, g_col, ALU.add, ALU.mult)
                i = (O_N2 if which else O_N1) if l < DEPTH else (O2_N2 if which else O2_N1)
                b, k = O.use(l, i)
                dve.wait_ge(o_full, 6 * l + (6 if which else 1))
                V.tensor_scalar(rs[:, 1, :], O.bank[b][:, 0:SEQ], 1.0 / D, EPS, ALU.mult, ALU.add).then_inc(O.read[b], 1)
                dve.wait_ge(x_root, n + 1)
                dve.drain()
                rsqrt(rs[:, 0, :], rs[:, 1, :], work[:, 0, 0:SEQ])
                for kt in range(KT):
                    stt(sq[:, kt, :], XT[:, kt, :], gain[:, kt:kt + 1], rs[:, 0, :], ALU.mult, ALU.mult).then_inc(h_scaled, 1)
                for kt in range(KT):
                    dve.wait_ge(h_hi_ready, n * KT + kt + 1)
                    if shift is None:
                        V.tensor_tensor(HL[:, kt, :], sq[:, kt, :], HH[:, kt, :].bitcast(f32), ALU.subtract).then_inc(h_ready, 1)
                    else:
                        stt(HL[:, kt, :], sq[:, kt, :], shift[:, kt:kt + 1], HH[:, kt, :].bitcast(f32),
                            ALU.add, ALU.subtract).then_inc(h_ready, 1)

            def bc3(ap, n, m):
                return ap.unsqueeze(1).to_broadcast([P, m, n])

            def rope(x, heads, tab, tt):
                n = heads * 32
                w = [work[:, i, 0:n].rearrange("p (h e) -> p h e", e=32) for i in range(3)]
                x1, x2 = x[:, :, 0:32], x[:, :, 32:64]
                t = [bc3(tab[i][:, tt, :], 32, heads) for i in range(4)]
                dve.drain()
                V.tensor_tensor(w[0], x1, t[0], ALU.mult)
                V.tensor_tensor(w[1], x2, t[1], ALU.mult)
                V.tensor_tensor(w[2], x2, t[2], ALU.mult)
                dve.drain()
                V.tensor_tensor(x2, x1, t[3], ALU.mult)
                dve.drain()
                V.tensor_tensor(x1, w[0], w[1], ALU.subtract)
                return V.tensor_tensor(x2, w[2], x2, ALU.add)

            def qk_norm(l, i, g_row):
                r = small[:, 64 + 32 * i:96 + 32 * i]
                for tt in range(TT):
                    x = qkv[:, i, tt, :]
                    for hf in range(2):
                        dve.drain()
                        V.tensor_tensor(work[:, hf, :], x[:, 512 * hf:512 * hf + 512], x[:, 512 * hf:512 * hf + 512], ALU.mult)
                        dve.drain()
                        V.tensor_reduce(out=r[:, 16 * tt + 8 * hf:16 * tt + 8 * hf + 8],
                                        in_=work[:, hf, :].rearrange("p (h e) -> p h e", e=HD), axis=AX.X, op=ALU.add)
                dve.drain()
                V.tensor_scalar(r, r, 1.0 / HD, EPS, ALU.mult, ALU.add).then_inc(qk_sum, 1)
                dve.wait_ge(qk_root, 2 * l + i + 1)
                r, v = root[:, i, :], r
                rsqrt(r, v, work[:, 0, 0:32])
                for tt in range(TT):
                    x = qkv[:, i, tt, :].rearrange("p (h e) -> p h e", e=HD)
                    a = V.tensor_tensor(x, x, r[:, 16 * tt:16 * tt + 16].unsqueeze(2).to_broadcast([P, HEADS, HD]), ALU.mult)
                return a

            def tables(g0):
                g1, g2_ = prm[:, g0:g0 + 32], prm[:, g0 + 32:g0 + 64]
                sn, cs = sc_tab[:, 0], sc_tab[:, 1]
                dve.drain()
                for i, (t, g) in enumerate(((cs, g1), (sn, g2_), (cs, g2_), (sn, g1))):
                    V.tensor_tensor(rt[:, i], t, bc3(g, 32, TT), ALU.mult)

            def softplus(x, u, n, sign):
                z, z2, s = small[:, 160:160 + n], work[:, 3, 0:n], work[:, 3, 64:64 + n]
                V.tensor_scalar(z2, u, 2.0, None, ALU.add)
                dve.drain()
                V.reciprocal(z2, z2)
                dve.drain()
                V.tensor_tensor(z, u, z2, ALU.mult)
                dve.drain()
                V.tensor_tensor(z2, z, z, ALU.mult)
                dve.drain()
                V.tensor_scalar(s, z2, 1.0 / 17, None, ALU.mult)
                for d in (15, 13, 11, 9, 7, 5, 3):
                    dve.drain()
                    stt(s, s, 1.0 / d, z2, ALU.add, ALU.mult)
                dve.drain()
                stt(s, s, 1.0, z, ALU.add, ALU.mult)
                V.tensor_scalar(x, x, 0.0, None, ALU.max)
                dve.drain()
                stt(x, s, 2.0, x, ALU.mult, ALU.add)
                dve.drain()
                if sign < 0:
                    V.tensor_scalar(x, x, -1.0, None, ALU.mult)
                    dve.drain()

            def turn_qk(l, t0):
                for r in range(1, 8, 2):
                    b, k = T.use(l, t0 + r)
                    dve.wait_ge(T.full[b], k + 1)
                    dst = qT if r < 4 else kT
                    j = 2 * (r % 4)
                    V.tensor_copy(dst[:, j:j + 2, :], T.bank[b][:]).then_inc(T.read[b], 1)

            def attention(l, bias_of):
                s0, t0, o0 = (S_AT, T_AT, O_AT) if l < DEPTH else (S2_AT, T2_AT, O2_AT)

                def turn_evac(h):
                    b, k = T.use(l, t0 + h)
                    dve.wait_ge(T.full[b], k + 1)
                    V.tensor_copy(probsT[:, h % 2, :], T.bank[b][:, 0:CW]).then_inc(T.read[b], 1)

                def normalise(q4):
                    b, k = O.use(l, o0 + q4)
                    dve.wait_ge(o_full, 6 * l + 2 + q4)
                    h0 = 4 * q4
                    V.reciprocal(row_inv[:, h0:h0 + 4, :], row_sum[:, h0:h0 + 4, :])
                    dve.drain()
                    for tt in range(TT):
                        o = O.bank[b][:].rearrange("p (h t d) -> p h t d", h=4, t=TT)[:, :, tt, :]
                        ins = V.tensor_tensor(o_tok[:, tt, 64 * h0:64 * h0 + 256].rearrange("p (h d) -> p h d", d=HD), o,
                                              row_inv[:, h0:h0 + 4, tt].unsqueeze(2).to_broadcast([P, 4, HD]), ALU.mult)
                    ins.then_inc(O.read[b], 1)

                for h in range(HEADS):
                    b, k = S.use(l, s0 + h)
                    dve.wait_ge(S.full[b], k + 1)
                    if h >= 2:
                        b2, k2 = T.use(l, t0 + h - 2)
                        dve.wait_ge(T.full[b2], k2 + 1)
                    bias = bias_of(h)
                    dve.drain()
                    for a, e, tt in ((0, P, 0), (P, CW, 1)):
                        ins = V.tensor_tensor_reduce(out=probs[:, h % 2, a:e], in0=S.bank[b][:, a:e], in1=bias[:, a:e], scale=1.0,
                                                     scalar=PICKED, op0=ALU.add, op1=ALU.max, accum_out=row_max[:, h, tt:tt + 1])
                    ins.then_inc(S.read[b], 1)
                    dve.drain()
                    V.tensor_scalar(neg_max[:, h, :], row_max[:, h, :], -SCALE, None, ALU.mult).then_inc(max_ready, 1)
                    if h >= 1 and (h - 1) % 2:
                        turn_evac(h - 1)
                    if h % 4 == 2 and h > 2:
                        normalise(h // 4 - 1)
                turn_evac(HEADS - 1)
                normalise(3)

            def turn_o(l, t0):
                for r in range(4):
                    b, k = T.use(l, t0 + r)
                    dve.wait_ge(oT_hi_ready, l * 4 + r + 1)
                    V.tensor_tensor(OTL[:, 2 * r:2 * r + 2, :], T.bank[b][:].rearrange("p (k t) -> p k t", k=2),
                                    OTH[:, 2 * r:2 * r + 2, :].bitcast(f32), ALU.subtract).then_inc(T.read[b], 1)

            def add_to_x(l, o, j, g_col):
                b, k = gemm_use(l, o)
                for i in range(2):
                    g = 1.0 if g_col is None else g_col[:, 2 * j + i:2 * j + i + 1]
                    ins = stt(XT[:, 2 * j + i, :], gemm[b][:, i * SEQ:(i + 1) * SEQ], g, XT[:, 2 * j + i, :], ALU.mult, ALU.add)
                ins.then_inc(gemm_read[b], 1)

            V.memset(ones[:], 1.0)
            V.memset(eps[:], EPS)
            V.memset(cs_row[:], 0.0)
            dve.wait_ge(in_full, 96)
            V.tensor_copy(ident_b[:], ident)
            V.tensor_copy(maskT_b[:], cst[:, slice(*CST["maskT"])]).then_inc(set_up, 1)
            V.tensor_copy(pos_f[:], pos_i[:])
            dve.drain()
            two_pi = (6.28125, float(np.float32(2 * math.pi - 6.28125)), float(2 * math.pi - 6.28125 - float(np.float32(2 * math.pi - 6.28125))))
            ang, turns = work[:, 0, 0:64], work[:, 1, 0:64]
            for tt in range(TT):
                V.tensor_scalar(ang[:, 32 * tt:32 * tt + 32], inv_freq, pos_f[:, tt:tt + 1], None, ALU.mult)
            magic = 1.5 * 2.0 ** 23
            for i, shift in ((0, 0.0), (1, 0.25)):
                r = sc_tab[:, i].rearrange("p t e -> p (t e)")
                dve.drain()
                V.tensor_scalar(turns, ang, 1.0 / (2 * math.pi), shift, ALU.mult, ALU.add)
                dve.drain()
                V.tensor_scalar(turns, turns, magic, None, ALU.add)
                dve.drain()
                V.tensor_scalar(turns, turns, magic, None, ALU.subtract)
                dve.drain()
                stt(r, turns, -two_pi[0], ang, ALU.mult, ALU.add)
                for part in two_pi[1:]:
                    dve.drain()
                    stt(r, turns, -part, r, ALU.mult, ALU.add)
                dve.drain()
                V.tensor_scalar(r, r, i * math.pi / 2, 3.1415925, ALU.add, ALU.min)
                dve.drain()
                V.tensor_scalar(r, r, -3.1415925, None, ALU.max)
            dve.drain().then_inc(sin_arg, 1)
            dve.wait_ge(c_ready, 1)
            stt(small[:, 0:KT], small[:, 0:KT], 1.0, c_act[:], ALU.add, ALU.mult)
            dve.drain()
            V.tensor_scalar(c_act[:], small[:, 0:KT], 0.5, None, ALU.mult)
            dve.drain()
            for g in range(2):
                for j in range(KT):
                    ada(ada_group(0, g), j)
                dve.drain().then_inc(ada_acc_ready, 1)
                mods(ada_group(0, g))

            def ada_done(grp):
                dve.drain().then_inc(ada_acc_ready, 1)

            for l in range(DEPTH):
                dve.wait_ge(prm_full, 16 * (l + 1))
                dve.drain()
                norm(l, 0, col("norm1", 0, KT), mod[:, l, 8:16], mod[:, l, 0:8])
                for u in range(U_IDX, U_Q):
                    b, k = gemm_use(l, u)
                    dve.wait_ge(chunk_done, unit_end(l, u))
                    src = gemm[b][:].rearrange("p (t n) -> p t n", t=TT)
                    if u < 2:
                        V.tensor_copy(iq[:, :, 256 * u:256 * u + 256], src).then_inc(gemm_read[b], 1)
                    elif u == 2:
                        V.tensor_copy(ik[:, :, 0:HD], src[:, :, 0:HD])
                        V.tensor_copy(iw[:], src[:, :, HD:HD + IDX_HEADS]).then_inc(gemm_read[b], 1)
                    else:
                        V.tensor_tensor(dt_s[:], src[:, :, 0:32], bc3(col("dtb", 0, 32), 32, TT), ALU.add).then_inc(gemm_read[b], 1)
                if l == 0:
                    dve.wait_ge(sin_done, 1)
                sn, cs = sc_tab[:, 0], sc_tab[:, 1]
                plain = (cs, sn, cs, sn)
                for tt in range(TT):
                    rope(ik[:, tt, 0:HD].rearrange("p (h e) -> p h e", e=HD), 1, plain, tt)
                dve.drain()
                V.tensor_copy(ik[:, :, HD:P], ik[:, :, 0:HD])
                for tt in range(TT):
                    ins = rope(iq[:, tt, :].rearrange("p (h e) -> p h e", e=HD), IDX_HEADS, plain, tt)
                dve.drain().then_inc(idx_rot, 1)
                for r in range(3):
                    b, k = T.use(l, T_IQ + r)
                    dve.wait_ge(T.full[b], k + 1)
                    dst = iqT[:, 2 * r:2 * r + 2, :] if r < 2 else ikT[:]
                    V.tensor_copy(dst, T.bank[b][:] if r < 2 else T.bank[b][:, 0:SEQ]).then_inc(T.read[b], 1)
                for h in range(IDX_HEADS):
                    b, k = S.use(l, S_IDX + h)
                    dve.wait_ge(S.read[b], k + 1)
                    for a, e, tt in ((0, P, 0), (P, CW, 1)):
                        if h == 0:
                            ins = V.tensor_scalar(idx_score[:, a:e], idx_relu[:, 0, a:e], iw[:, tt, 0:1], None, ALU.mult)
                        else:
                            ins = stt(idx_score[:, a:e], idx_relu[:, h % 2, a:e], iw[:, tt, h:h + 1], idx_score[:, a:e],
                                      ALU.mult, ALU.add)
                    ins.then_inc(relu_used, 1)
                    dve.drain()
                stt(idx_score[:], idx_score[:], IDX_SCALE, causal, ALU.mult, ALU.add)
                for i in range(TOP8):
                    src = idx_left if i else idx_score
                    dve.drain()
                    for a, e, tt in ((0, P, 0), (P, CW, 1)):
                        V.max(small[:, 8 * tt:8 * tt + 8], src[:, a:e])
                    dve.drain()
                    for a, e, tt in ((0, P, 0), (P, CW, 1)):
                        V.match_replace(out=idx_left[:, a:e], in_to_replace=small[:, 8 * tt:8 * tt + 8], in_values=src[:, a:e],
                                        imm_value=PICKED)
                dve.drain()
                V.tensor_scalar(keep_bias[:], idx_left[:], -2e38, NEG, ALU.is_gt, ALU.mult)
                dve.drain()
                V.tensor_tensor(keep_bias[:], keep_bias[:], causal, ALU.add)
                for i in range(2):
                    for b in range(2):
                        k = gemm_use(l, U_Q + 4 * i + 2 + b)[1]
                        dve.wait_ge(gemm_read[b], k + 1)
                    tables(PRM["qg"][0] if i == 0 else PRM["kg"][0])
                    qk_norm(l, i, None)
                    for tt in range(TT):
                        rope(qkv[:, i, tt, :].rearrange("p (h e) -> p h e", e=HD), HEADS, [rt[:, q] for q in range(4)], tt)
                    dve.drain().then_inc(qk_rot, 1)
                d2 = dt_s[:].rearrange("p t h -> p (t h)")
                stt(small[:, 0:64], d2, -1.0, d2, ALU.mult, ALU.min).then_inc(sp_in, 1)
                dve.wait_ge(sp_exp, 2 * l + 2)
                softplus(d2, small[:, 0:64], 64, 1)
                ins = V.scalar_tensor_tensor(out=small[:, 0:64].rearrange("p (t h) -> p t h", t=TT), in0=dt_s[:], scalar=-1.0,
                                             in1=bc3(small[:, 128:160], 32, TT), op0=ALU.mult, op1=ALU.mult).then_inc(a_ready, 1)
                b, k = T.use(l, T_A)
                dve.wait_ge(T.full[b], k + 1)
                V.tensor_copy(a_row[:], T.bank[b][0:32, 0:SEQ]).then_inc(T.read[b], 1)
                dve.drain()
                V.tensor_tensor_scan(out=cs_row[0:32, :], data0=ones[0:32, :], data1=a_row[:], initial=0.0,
                                     op0=ALU.mult, op1=ALU.add).then_inc(cs_ready, 1)
                for u in range(U_XBC, U_GA):
                    v = u - U_XBC
                    b, k = gemm_use(l, u)
                    dve.wait_ge(conv_first, l * 24 + 2 * v + 2)
                    for d in range(1, SSM_CONV):
                        if d > 1:
                            dve.drain()
                        for j in range(2):
                            o = j * SEQ
                            c = conv[:, v % 2, o + d:o + SEQ]
                            ins = stt(c, gemm[b][:, o:o + SEQ - d], col("convw", (3 - d) * XBC_TILES + 2 * v + j), c, ALU.mult, ALU.add)
                    ins.then_inc(gemm_read[b], 1)
                    dve.drain()
                b, k = T.use(l, T_CS)
                dve.wait_ge(T.full[b], k + 1)
                V.tensor_scalar(neg_cs[:], T.bank[b][:, 0:64].rearrange("p (t h) -> p t h", t=TT), -1.0, None, ALU.mult
                                ).then_inc(T.read[b], 1)
                dve.drain().then_inc(ncs_ready, 1)
                turn_qk(l, T_QK)
                attention(l, lambda h: keep_bias)
                dve.drain().then_inc(o_ready, 1)
                turn_o(l, T_OT)
                dve.drain().then_inc(oT_ready, 1)
                for u in range(U_GA, U_AO):
                    g, j = (u - U_GA) // 4, (u - U_GA) % 4
                    if j == 0 and g:
                        mods(ada_group(l, 1 + g))
                    ada(ada_group(l, 2 + g), 2 * j)
                    ada(ada_group(l, 2 + g), 2 * j + 1)
                    if j == 3:
                        ada_done(0)
                for u in range(U_AO, U_SO):
                    j = u - U_AO
                    b, k = gemm_use(l, u)
                    dve.wait_ge(chunk_done, unit_end(l, u))
                    V.tensor_tensor(gates[:, 0, 2 * j:2 * j + 2, :], gemm[b][:].rearrange("p (k t) -> p k t", k=2),
                                    gates[:, 0, 2 * j:2 * j + 2, :], ALU.mult).then_inc(gemm_read[b], 1)
                    if j == 0:
                        mods(ada_group(l, 3))
                    ada(ada_group(l, 4), 2 * j)
                    ada(ada_group(l, 4), 2 * j + 1)
                    if j == 3:
                        ada_done(0)
                for g in range(SSM_GROUPS):
                    b, k = S.use(l, S_CB + g)
                    dve.wait_ge(S.full[b], k + 1)
                    V.tensor_copy(CB[:, g, :], S.bank[b][:, 0:CW]).then_inc(S.read[b], 1)
                for hf in range(2):
                    tx, ts = t_half(hf)
                    if hf:
                        dve.wait_ge(y_done, l * 32 + 16)
                    for r in range(4):
                        b, k = T.use(l, tx + r)
                        dve.wait_ge(T.full[b], k + 1)
                        h0 = 16 * hf + 4 * r
                        for tt in range(TT):
                            ins = V.tensor_tensor(xdt[:, tt, 256 * r:256 * r + 256].rearrange("p (h d) -> p h d", d=HD),
                                                  T.bank[b][:, 256 * tt:256 * tt + 256].rearrange("p (h d) -> p h d", d=HD),
                                                  dt_s[:, tt, h0:h0 + 4].unsqueeze(2).to_broadcast([P, 4, HD]), ALU.mult)
                        ins.then_inc(T.read[b], 1)
                    dve.drain()
                    for h in range(16 * hf, 16 * hf + 16):
                        b, k = S.use(l, S_SSM + h)
                        n = l * 32 + h
                        dve.wait_ge(S.read[b], k + 1)
                        if n >= 2:
                            dve.wait_ge(y_done, n - 1)
                        V.tensor_tensor(probsT[:, h % 2, :], probs[:, b, :], CB[:, h // 8, :], ALU.mult).then_inc(g_ready, 1)
                        if h % 2 and h > 16 * hf + 1:
                            f = h // 2 - 1
                            b2, k2 = O.use(l, O_Y + f)
                            dve.wait_ge(y_done, l * 32 + 2 * f + 2)
                            stt(work[:, f % 2, 0:SEQ], xs[:, f, :], col("skip", f), O.bank[b2][:, 0:SEQ], ALU.mult, ALU.add
                                ).then_inc(O.read[b2], 1)
                            dve.drain()
                            V.tensor_tensor(zg[:, f, :], work[:, f % 2, 0:SEQ], zg[:, f, :], ALU.mult).then_inc(y_gated, 1)
                    f = 8 * hf + 7
                    b2, k2 = O.use(l, O_Y + f)
                    dve.wait_ge(y_done, l * 32 + 2 * f + 2)
                    stt(work[:, f % 2, 0:SEQ], xs[:, f, :], col("skip", f), O.bank[b2][:, 0:SEQ], ALU.mult, ALU.add
                        ).then_inc(O.read[b2], 1)
                    dve.drain()
                    V.tensor_tensor(zg[:, f, :], work[:, f % 2, 0:SEQ], zg[:, f, :], ALU.mult).then_inc(y_gated, 1)
                    for gi in range(2):
                        b, k = T.use(l, ts + gi)
                        dve.wait_ge(T.full[b], k + 1)
                        V.tensor_scalar(work[:, gi, 0:SEQ], T.bank[b][:, 0:SEQ], 1.0 / 512, EPS, ALU.mult, ALU.add
                                        ).then_inc(T.read[b], 1)
                    dve.wait_ge(y_root, 4 * l + 2 * hf + 2)
                    dve.drain()
                    rsqrt(rs[:, 0:2, :], work[:, 0:2, 0:SEQ], work[:, 2:4, 0:SEQ])
                    for f in range(8):
                        t = 8 * hf + f
                        stt(zg[:, t, :], zg[:, t, :], col("ssmn", t), rs[:, f // 4, :], ALU.mult, ALU.mult).then_inc(y_scaled, 1)
                    for f in range(8):
                        n = l * 16 + 8 * hf + f
                        dve.wait_ge(y_hi, n + 1)
                        V.tensor_tensor(OTL[:, f, :], zg[:, 8 * hf + f, :], OTH[:, f, :].bitcast(f32), ALU.subtract
                                        ).then_inc(y_ready, 1)
                    for u in range(U_SO + 4 * hf, U_SO + 4 * hf + 4):
                        j = (u - U_SO) % 4
                        b, k = gemm_use(l, u)
                        dve.wait_ge(chunk_done, unit_end(l, u))
                        dve.drain()
                        V.tensor_tensor(work[:, j % 2, :], gemm[b][:], gates[:, 1, 2 * j:2 * j + 2, :].rearrange("p k t -> p (k t)"),
                                        ALU.mult).then_inc(gemm_read[b], 1)
                        dve.drain()
                        mx = gates[:, 0, 2 * j:2 * j + 2, :].rearrange("p k t -> p (k t)")
                        ins = V.tensor_tensor(mx, work[:, j % 2, :], mx, ALU.add)
                        if hf:
                            ins.then_inc(mix_ready, 1)
                        if j == 0:
                            mods(ada_group(l, 4 + hf))
                        if hf == 0:
                            ada(ada_group(l, 5), 2 * j)
                            ada(ada_group(l, 5), 2 * j + 1)
                            if j == 3:
                                ada_done(0)
                for j in range(4):
                    dve.wait_ge(mix_hi, l * 4 + j + 1)
                    V.tensor_tensor(HL[:, 2 * j:2 * j + 2, :], gates[:, 0, 2 * j:2 * j + 2, :],
                                    HH[:, 2 * j:2 * j + 2, :].bitcast(f32), ALU.subtract).then_inc(mix_low, 1)
                for j in range(4):
                    dve.wait_ge(chunk_done, unit_end(l, U_OUT + j))
                    add_to_x(l, U_OUT + j, j, mod[:, l, 16:24])
                norm(l, 1, col("norm2", 0, KT), mod[:, l, 32:40], mod[:, l, 24:32])
                for u in range(U_UP, U_DN):
                    i = u - U_UP
                    n = l * FT + i
                    b, k = gemm_use(l, u)
                    dve.wait_ge(up_first, n + 1)
                    for d in range(1, FFN_CONV):
                        if d > 1:
                            dve.drain()
                        for j in range(2):
                            o = j * SEQ
                            c = conv[:, i % 2, o + d:o + SEQ]
                            ins = stt(c, gemm[b][:, o:o + SEQ - d], col("ffnw", (2 - d) * 2 * FT + j * FT + i), c, ALU.mult, ALU.add)
                    ins.then_inc(gemm_read[b], 1)
                    dve.wait_ge(up_silu, n + 1)
                    dve.drain()
                    V.tensor_tensor(work[:, i % 2, 0:SEQ], work[:, i % 2, 0:SEQ], conv[:, i % 2, 0:SEQ], ALU.mult).then_inc(up_prod, 1)
                    if l + 1 < DEPTH:
                        if i == KT:
                            mods(ada_group(l + 1, 0))
                        if i < 2 * KT:
                            ada(ada_group(l + 1, i // KT), i % KT)
                            if i % KT == KT - 1:
                                ada_done(0)
                        if i == 2 * KT:
                            mods(ada_group(l + 1, 1))
                    dve.wait_ge(up_hi, n + 1)
                    V.tensor_tensor(FL[:, i, :], work[:, i % 2, 0:SEQ], FH[:, i, :].bitcast(f32), ALU.subtract).then_inc(up_ready, 1)
                dve.drain()
                for j in range(4):
                    dve.wait_ge(chunk_done, l * NCH + 2 * U_DN + (j + 1) * DN_CHUNKS)
                    add_to_x(l, U_DN + j, j, mod[:, l, 40:48])
                dve.drain()

            l = DEPTH
            norm(l, 0, prm2[:, 0:KT], None, None)
            dve.wait_ge(tab_full, 32)
            for i in range(2):
                for b in range(2):
                    k = gemm_use(l, 4 * i + 2 + b)[1]
                    dve.wait_ge(gemm_read[b], k + 1)
                qk_norm(l, i, None)
                dve.drain()
                x = qkv[:, i]
                V.tensor_tensor(x, x, bc3(rows2_sb[:, i, :], D, TT), ALU.mult)
                dve.drain().then_inc(qk_rot, 1)
            b, k = gemm_use(l, V_G)
            dve.wait_ge(gemm_read[b], k + 1)
            n_f = TT * N_FOX
            nf = small[:, 226:226 + n_f]
            V.tensor_tensor(nf.rearrange("p (t h) -> p t h", t=TT), g2[:, :, 0:N_FOX], bc3(prm2[:, 2 * KT:], N_FOX, TT), ALU.add)
            dve.drain()
            stt(small[:, 0:n_f], nf, -1.0, nf, ALU.mult, ALU.min)
            V.tensor_scalar(small[:, 240:240 + n_f], nf, -1.0, None, ALU.mult)
            dve.drain().then_inc(sp_in, 1)
            dve.wait_ge(sp_exp, 2 * l + 1)
            softplus(small[:, 240:240 + n_f], small[:, 0:n_f], n_f, -1)
            dve.drain().then_inc(a_ready, 1)
            b, k = T.use(l, T2_A)
            dve.wait_ge(T.full[b], k + 1)
            V.tensor_copy(a_row[0:N_FOX, :], T.bank[b][0:N_FOX, 0:SEQ]).then_inc(T.read[b], 1)
            dve.drain()
            V.tensor_tensor_scan(out=cs_row[0:N_FOX, :], data0=ones[0:N_FOX, :], data1=a_row[0:N_FOX, :], initial=0.0,
                                 op0=ALU.mult, op1=ALU.add).then_inc(cs_ready, 1)
            for i in range(N_FOX):
                b, k = S.use(l, S2_FOX + i)
                dve.wait_ge(S.full[b], k + 1)
                stt(fox_bias[:, i, 0:P], S.bank[b][:, 0:P], -1.0 / SCALE, causal[:, 0:P], ALU.mult, ALU.add)
                stt(fox_bias[:, i, P:CW], S.bank[b][:, 0:SEQ], -1.0 / SCALE, causal[:, P:CW], ALU.mult, ALU.add
                    ).then_inc(S.read[b], 1)
            turn_qk(l, T2_QK)
            fox_end = N_MOBA + N_FOX

            def bias2(h):
                if h < N_MOBA:
                    return alibi_sb[:, h, :]
                if h < fox_end:
                    return fox_bias[:, h - N_MOBA, :]
                return alibi_sb[:, h - N_FOX, :]

            attention(l, bias2)
            spans = ((0, N_MOBA * HD), (N_MOBA * HD, fox_end * HD), (fox_end * HD, D))
            for tt in range(TT):
                for i, (a, e) in enumerate(spans):
                    w = work[:, i, 0:e - a]
                    dve.drain()
                    V.tensor_tensor(w, o_tok[:, tt, a:e], o_tok[:, tt, a:e], ALU.mult)
                    dve.drain()
                    V.tensor_reduce(out=small[:, 3 * tt + i:3 * tt + i + 1], in_=w, axis=AX.X, op=ALU.add)
            dve.drain()
            for tt in range(TT):
                for i, (a, e) in enumerate(spans):
                    r = small[:, 3 * tt + i:3 * tt + i + 1]
                    V.tensor_scalar(r, r, 1.0 / (e - a), EPS, ALU.mult, ALU.add)
            dve.drain().then_inc(og_in, 1)
            dve.wait_ge(og_root, 1)
            rsqrt(root[:, 2, 0:6], small[:, 0:6], work[:, 0, 0:6])
            for tt in range(TT):
                for i, (a, e) in enumerate(spans):
                    stt(o_tok[:, tt, a:e], o_tok[:, tt, a:e], root[:, 2, 3 * tt + i:3 * tt + i + 1], rows2_sb[:, 2, a:e],
                        ALU.mult, ALU.mult)
            dve.drain()
            a, e = spans[1]
            V.tensor_tensor(o_tok[:, :, a:e], o_tok[:, :, a:e], g2[:, :, N_FOX:], ALU.mult)
            dve.drain().then_inc(o_ready, 1)
            turn_o(l, T2_OT)
            dve.drain().then_inc(oT_ready, 1)
            for j in range(4):
                dve.wait_ge(chunk_done, unit_end(l, V_OUT + j))
                add_to_x(l, V_OUT + j, j, None)
            norm(l, 1, prm2[:, KT:2 * KT], None, None)
            for u in range(V_UP, V_DN):
                i = u - V_UP
                n = DEPTH * FT + i
                b, k = gemm_use(l, u)
                dve.wait_ge(up_first, n + 1)
                stt(work[:, i % 2, :], gemm[b][:], 0.0, conv[:, i % 2, :], ALU.max, ALU.mult).then_inc(gemm_read[b], 1)
                dve.wait_ge(up_hi, n + 1)
                V.tensor_tensor(F2L[:, 2 * i:2 * i + 2, :].rearrange("p k t -> p (k t)"), work[:, i % 2, :],
                                F2H[:, 2 * i:2 * i + 2, :].rearrange("p k t -> p (k t)").bitcast(f32), ALU.subtract
                                ).then_inc(up_ready, 1)
            for j in range(4):
                dve.wait_ge(chunk_done, DEPTH * NCH + 2 * V_DN + (j + 1) * DN2_CHUNKS)
                add_to_x(l, V_DN + j, j, None)

        @block.tensor
        def _(pe):
            M = nc.tensor.matmul

            def products(passes, first, last):
                for i, (o, a, b) in enumerate(passes):
                    ins = M(o, a, b, start=first and i == 0, stop=last and i == len(passes) - 1, skip_group_check=True)
                return ins

            def weights(g):
                pe.wait_ge(hi_ready, g + 1)
                pe.wait_ge(lo_ready, g + 1)
                l = min(g // NCH, DEPTH)
                return g % RING, chunk_words(l, g - l * NCH)

            def feature_chunk(g, out, xh, xl, k0, first, last):
                s, n = weights(g)
                kts = n // 256
                wh = w_hi[:, s, 0:n].rearrange("p (k n) -> p k n", n=256)
                wl = w_lo[:, s, 0:n].rearrange("p (k n) -> p k n", n=256)
                passes = []
                for j in range(2):
                    o = out[:, j * SEQ:(j + 1) * SEQ]
                    c = slice(j * P, (j + 1) * P)
                    for k in range(kts):
                        passes += [(o, wh[:, k, c], xh[:, k0 + k, :]), (o, wh[:, k, c], xl[:, k0 + k, :]),
                                   (o, wl[:, k, c], xh[:, k0 + k, :])]
                products(passes, first, last).then_inc(chunk_done, 1)

            def token_chunk(g, out, xh, xl, k0, first, last):
                s, n = weights(g)
                w = n // 4
                wh = w_hi[:, s, 0:n].rearrange("p (k n) -> p k n", k=4)
                wl = w_lo[:, s, 0:n].rearrange("p (k n) -> p k n", k=4)
                passes = []
                for j in range(TT):
                    o = out[:, j * 256:j * 256 + w]
                    c = slice(j * P, (j + 1) * P)
                    for k in range(4):
                        passes += [(o, xh[:, k0 + k, c], wh[:, k, :]), (o, xh[:, k0 + k, c], wl[:, k, :]),
                                   (o, xl[:, k0 + k, c], wh[:, k, :])]
                products(passes, first, last).then_inc(chunk_done, 1)

            def free_gemm(l, o):
                b, k = gemm_use(l, o)
                if k:
                    pe.wait_ge(gemm_read[b], k)
                return gemm[b]

            def unit(l, u, chunk, xh, xl):
                out = free_gemm(l, u)
                g = first_chunk(l, u)
                chunk(g, out, xh, xl, 0, True, False)
                chunk(g + 1, out, xh, xl, 4, False, True)

            def take(pair, l, i):
                b, k = pair.use(l, i)
                if k:
                    pe.wait_ge(pair.read[b], k)
                return b, pair.bank[b]

            def arrived(pair, l, i):
                b, k = pair.use(l, i)
                pe.wait_ge(pair.read[b], k + 1)

            def ada_sums(grp):
                pe.wait_ge(ada_acc_ready, grp + 1)
                if grp:
                    pe.wait_ge(mod_ready, grp)
                for t in range(KT):
                    ins = M(mod_ps[:, t:t + 1], ada_acc[:, t * P:(t + 1) * P], ones[:, 0:1], start=True, stop=True)
                ins.then_inc(ada_sum, 1)

            def norm_sum(l, which):
                i = (O_N2 if which else O_N1) if l < DEPTH else (O2_N2 if which else O2_N1)
                b, out = take(O, l, i)
                for kt in range(KT):
                    if kt % 2 == 0:
                        pe.wait_ge(sq_ready, (2 * l + which) * 4 + kt // 2 + 1)
                    ins = M(out[:, 0:SEQ], ones[:, 0:P], sq[:, kt, :], start=kt == 0, stop=kt == KT - 1)
                ins.then_inc(o_full, 1)
                pe.wait_ge(h_ready, (2 * l + which + 1) * KT)

            def turn(l, i, blocks):
                b, out = take(T, l, i)
                for c, rows, src, n in blocks:
                    ins = nc.tensor.transpose(out[0:rows, c:c + n], src, ident[0:n, 0:n])
                ins.then_inc(T.full[b], 1)

            def turn_tokens(l, t0, src_of, rounds):
                for r in range(rounds):
                    src = src_of(r)
                    turn(l, t0 + r, [(j * SEQ + tt * P, P, src[:, tt, j * P:(j + 1) * P], P)
                                     for j in range(2) for tt in range(TT)])

            def attention(l):
                s0, t0, o0 = (S_AT, T_AT, O_AT) if l < DEPTH else (S2_AT, T2_AT, O2_AT)

                def scores(h):
                    b, out = take(S, l, s0 + h)
                    r = slice(64 * (h % 2), 64 * (h % 2) + 64)
                    M(out[:, 0:P], qT[r, h // 2, 0:P], kT[r, h // 2, 0:P], start=True, stop=True)
                    M(out[:, P:CW], qT[r, h // 2, P:SEQ], kT[r, h // 2, :], start=True, stop=True).then_inc(S.full[b], 1)

                def values(h):
                    arrived(T, l, t0 + h)
                    i = o0 + h // 4
                    b, k = O.use(l, i)
                    if h % 4 == 0:
                        take(O, l, i)
                    c = (h % 4) * P
                    v = qkv[:, 2, :, h * HD:(h + 1) * HD]
                    pT = probsT[:, h % 2, :]
                    M(O.bank[b][:, c:c + HD], pT[:, 0:P], v[:, 0, :], start=True, stop=True)
                    M(O.bank[b][:, c + HD:c + P], pT[:, P:2 * P], v[:, 0, :], start=True, stop=False)
                    ins = M(O.bank[b][:, c + HD:c + P], pT[:, 2 * P:CW], v[:, 1, :], start=False, stop=True)
                    if h % 4 == 3:
                        ins.then_inc(o_full, 1)

                scores(0)
                for h in range(HEADS):
                    if h + 1 < HEADS:
                        scores(h + 1)
                    pe.wait_ge(exp_done, l * HEADS + h + 1)
                    turn(l, t0 + h, [(c, P, probs[:, h % 2, c:c + P], P) for c in (0, P, 2 * P)])
                    if h:
                        values(h - 1)
                values(HEADS - 1)

            pe.wait_ge(set_up, 1)
            for g in range(2):
                ada_sums(ada_group(0, g))
            for l in range(DEPTH):
                norm_sum(l, 0)
                for u in range(U_IDX, U_KV):
                    unit(l, u, token_chunk, HH, HL)
                pe.wait_ge(idx_rot, l + 1)
                turn_tokens(l, T_IQ, lambda r: iq[:, :, 256 * r:256 * r + 256], 2)
                turn(l, T_IQ + 2, [(tt * P, P, ik[:, tt, :], P) for tt in range(TT)])
                for r in range(3):
                    arrived(T, l, T_IQ + r)
                for h in range(IDX_HEADS):
                    b, o = take(S, l, S_IDX + h)
                    r = slice(64 * (h % 2), 64 * (h % 2) + 64)
                    M(o[:, 0:P], iqT[r, h // 2, 0:P], ikT[r, 0:P], start=True, stop=True)
                    M(o[:, P:CW], iqT[r, h // 2, P:SEQ], ikT[r, :], start=True, stop=True).then_inc(S.full[b], 1)
                for u in range(U_KV, U_Z):
                    unit(l, u, token_chunk, HH, HL)
                for u in range(U_Z, U_XBC):
                    unit(l, u, feature_chunk, HH, HL)
                pe.wait_ge(a_ready, l + 1)
                turn(l, T_A, [(tt * P, 32, small[:, 32 * tt:32 * tt + 32], P) for tt in range(TT)])
                for u in range(U_XBC, U_GA):
                    unit(l, u, feature_chunk, HH, HL)
                pe.wait_ge(cs_ready, l + 1)
                b, o = take(T, l, T_CS)
                for tt in range(TT):
                    ins = nc.tensor.transpose(o[:, 32 * tt:32 * tt + 32], cs_row[0:32, tt * P:(tt + 1) * P], ident[0:32, 0:32])
                ins.then_inc(T.full[b], 1)
                pe.wait_ge(qk_rot, 2 * l + 2)
                turn_tokens(l, T_QK, lambda r: qkv[:, r // 4, :, 256 * (r % 4):256 * (r % 4) + 256], 8)
                for r in range(6, 8):
                    arrived(T, l, T_QK + r)
                attention(l)
                pe.wait_ge(o_ready, l + 1)
                turn_tokens(l, T_OT, lambda r: o_tok[:, :, 256 * r:256 * r + 256], 4)
                for u in range(U_GA, U_AO):
                    unit(l, u, feature_chunk, HH, HL)
                    if u == U_GM:
                        ada_sums(ada_group(l, 2))
                pe.wait_ge(oT_ready, l + 1)
                for u in range(U_AO, U_SO):
                    unit(l, u, feature_chunk, OTH, OTL)
                    if u == U_AO:
                        ada_sums(ada_group(l, 3))
                pe.wait_ge(conv_act, (l + 1) * 12)
                for g in range(SSM_GROUPS):
                    b, o = take(S, l, S_CB + g)
                    M(o[:, 0:SEQ], bc[:, g, 0:P], bc[:, SSM_GROUPS + g, :], start=True, stop=True)
                    M(o[:, SEQ:CW], bc[:, g, P:SEQ], bc[:, SSM_GROUPS + g, P:SEQ], start=True, stop=True).then_inc(S.full[b], 1)

                def decay_exponents(h):
                    b, o = take(S, l, S_SSM + h)
                    pick = ident[:, h:h + 1].to_broadcast([P, P])
                    ins = products([(o[:, 0:SEQ], pick, cs_row[:, :]), (o[:, SEQ:CW], pick, cs_row[:, P:SEQ]),
                                    (o[:, 0:P], ident_b[:], maskT_b[:]), (o[:, SEQ:CW], ident_b[:], maskT_b[:])], True, True)
                    ins.then_inc(S.full[b], 1)

                def head_y(h):
                    pe.wait_ge(g_ready, l * 32 + h + 1)
                    b, k = O.use(l, O_Y + h // 2)
                    if h % 2 == 0:
                        take(O, l, O_Y + h // 2)
                    r = slice(64 * (h % 2), 64 * (h % 2) + 64)
                    c = (h % 16) * HD
                    M(O.bank[b][r, 0:SEQ], xdt[:, 0, c:c + HD], probsT[:, h % 2, 0:SEQ], start=True, stop=False)
                    M(O.bank[b][r, P:SEQ], xdt[:, 1, c:c + HD], probsT[:, h % 2, SEQ:CW], start=False, stop=True).then_inc(y_done, 1)

                for hf in range(2):
                    tx, ts = t_half(hf)
                    for r in range(4):
                        turn(l, tx + r, [(tt * SEQ + j * P, P, xs[:, 8 * hf + 2 * r + j, tt * P:(tt + 1) * P], P)
                                         for tt in range(TT) for j in range(2)])

                    def square_sum(f):
                        b, k = T.use(l, ts + (f % 8) // 4)
                        if f % 4 == 0:
                            take(T, l, ts + (f % 8) // 4)
                        pe.wait_ge(y_sq, l * 16 + f + 1)
                        ins = M(T.bank[b][:, 0:SEQ], ones[:, 0:P], work[:, f % 4, SEQ:2 * SEQ], start=f % 4 == 0, stop=f % 4 == 3)
                        if f % 4 == 3:
                            ins.then_inc(T.full[b], 1)

                    h0 = 16 * hf
                    decay_exponents(h0)
                    for r in range(2, 4):
                        arrived(T, l, tx + r)
                    for h in range(h0, h0 + 16):
                        if h + 1 < h0 + 16:
                            decay_exponents(h + 1)
                        head_y(h)
                        if h % 2 == 0 and h >= h0 + 4:
                            square_sum(h // 2 - 2)
                    square_sum(8 * hf + 6)
                    square_sum(8 * hf + 7)
                    if hf:
                        ada_sums(ada_group(l, 5))
                    pe.wait_ge(y_ready, l * 16 + 8 * hf + 8)
                    for u in range(U_SO + 4 * hf, U_SO + 4 * hf + 4):
                        unit(l, u, feature_chunk, OTH, OTL)
                        if u == U_SO:
                            ada_sums(ada_group(l, 4))
                pe.wait_ge(mix_low, 4 * (l + 1))
                for u in range(U_OUT, U_UP):
                    unit(l, u, feature_chunk, HH, HL)
                norm_sum(l, 1)
                for u in range(U_UP, U_DN):
                    unit(l, u, feature_chunk, HH, HL)
                    if l + 1 < DEPTH and u in (U_UP + KT, U_UP + 2 * KT):
                        ada_sums(ada_group(l + 1, (u - U_UP) // KT - 1))
                pe.wait_ge(up_ready, (l + 1) * FT)
                for j in range(4):
                    out_b = free_gemm(l, U_DN + j)
                    for c in range(DN_CHUNKS):
                        feature_chunk(l * NCH + 2 * U_DN + j * DN_CHUNKS + c, out_b, FH, FL, 4 * c, c == 0, c == DN_CHUNKS - 1)

            l = DEPTH
            norm_sum(l, 0)
            for u in range(0, V_OUT):
                unit(l, u, token_chunk, HH, HL)
            pe.wait_ge(a_ready, l + 1)
            turn(l, T2_A, [(tt * P, N_FOX, small[:, 240 + N_FOX * tt:240 + N_FOX * (tt + 1)], P) for tt in range(TT)])
            pe.wait_ge(qk_rot, 2 * l + 2)
            pe.wait_ge(cs_ready, l + 1)
            for i in range(N_FOX):
                b, o = take(S, l, S2_FOX + i)
                M(o[:, 0:SEQ], ident[:, i:i + 1].to_broadcast([P, P]), cs_row[:, :], start=True, stop=True).then_inc(S.full[b], 1)
            turn_tokens(l, T2_QK, lambda r: qkv[:, r // 4, :, 256 * (r % 4):256 * (r % 4) + 256], 8)
            for r in range(6, 8):
                arrived(T, l, T2_QK + r)
            attention(l)
            pe.wait_ge(o_ready, l + 1)
            turn_tokens(l, T2_OT, lambda r: o_tok[:, :, 256 * r:256 * r + 256], 4)
            pe.wait_ge(oT_ready, l + 1)
            for u in range(V_OUT, V_UP):
                unit(l, u, feature_chunk, OTH, OTL)
            norm_sum(l, 1)
            for u in range(V_UP, V_DN):
                unit(l, u, feature_chunk, HH, HL)
            pe.wait_ge(up_ready, DEPTH * FT + V_DN - V_UP)
            for j in range(4):
                out_b = free_gemm(l, V_DN + j)
                for c in range(DN2_CHUNKS):
                    feature_chunk(l * NCH + 2 * V_DN + j * DN2_CHUNKS + c, out_b, F2H, F2L, 4 * c, c == 0, c == DN2_CHUNKS - 1)


def shape_constants():
    t, s = np.arange(SEQ)[:, None], np.arange(SEQ)[None, :]

    def blocks(a):
        return np.concatenate([a[0:P, 0:P], a[P:SEQ, 0:SEQ]], axis=1)

    causal = np.where(s <= t, 0.0, NEG)
    inv = np.float32(1.0) / (10000.0 ** (np.arange(0, HD, 2) / HD)).astype(np.float32)
    consts = np.concatenate([np.eye(P), blocks(causal), causal[0:P, 0:P].T, np.tile(inv[None], (P, 1))], axis=1)
    n_alibi = N_MOBA + N_DIL
    slopes = 2.0 ** (-8.0 * np.arange(1, n_alibi + 1) / n_alibi)
    dist = t - s
    seen = (dist <= 128) * 1.0 + (dist % 4 == 0) + (dist % 16 == 0)
    alibi = []
    for h in range(N_MOBA):
        alibi.append(blocks(np.where(s <= t, -slopes[N_DIL + h] * dist / SCALE, NEG)))
    for h in range(N_DIL):
        alibi.append(blocks(np.where((s <= t) & (seen > 0), (np.log(np.maximum(seen, 1.0)) - slopes[h] * dist) / SCALE, NEG)))
    return consts.astype(np.float32), np.stack(alibi, axis=1).astype(np.float32)


def stream_of(w_in, w_attn_o, w_ssm_o, w_out, w_up, w_down, w_in_2, w_out_2, w_up_2, w_down_2):
    parts = []

    def chunk(w, row_tile, kts, c0, width):
        a = w[row_tile * P:(row_tile + kts) * P, c0:c0 + width]
        parts.append(a.reshape(kts, P, width).transpose(1, 0, 2).reshape(-1))

    def unit(w, c0, width=256, row_tile=0):
        chunk(w, row_tile, 4, c0, width)
        chunk(w, row_tile + 4, 4, c0, width)

    q, k, v, iq, ik, iw, z, xbc, dt, ga, gm, end = np.cumsum(
        [0, D, D, D, IDX_HEADS * HD, HD, IDX_HEADS, D_INNER, XBC_TILES * P, SSM_HEADS, D, D]).tolist()
    for l in range(DEPTH):
        w = w_in[l]
        for c in (iq, iq + 256):
            unit(w, c)
        unit(w, ik, HD + IDX_HEADS)
        unit(w, dt, SSM_HEADS)
        for a, e in ((q, iq), (z, xbc), (xbc, dt), (ga, gm), (gm, end)):
            for c in range(a, e, 256):
                unit(w, c)
        for c in range(0, D, 256):
            unit(w_attn_o[l], c)
        for hf in range(2):
            for c in range(0, D, 256):
                unit(w_ssm_o[l], c, 256, KT * hf)
        for c in range(0, D, 256):
            unit(w_out[l], c)
        up = w_up[l].reshape(D, 2, FT, P).transpose(0, 2, 1, 3).reshape(D, 2 * D_FF)
        for i in range(FT):
            unit(up, 256 * i)
        for c in range(0, D, 256):
            for i in range(DN_CHUNKS):
                chunk(w_down[l], 4 * i, min(4, FT - 4 * i), c, 256)
    w = w_in_2[0]
    for c in range(0, 3 * D, 256):
        unit(w, c)
    unit(w, 3 * D)
    unit(w, 3 * D + 256, G_COLS - 256)
    for c in range(0, D, 256):
        unit(w_out_2[0], c)
    for c in range(0, D_FF2, 256):
        unit(w_up_2[0], c)
    for c in range(0, D, 256):
        for i in range(DN2_CHUNKS):
            chunk(w_down_2[0], 4 * i, 4, c, 256)
    return np.concatenate(parts)


def kernel(x, c, positions, w_ada, b_ada, norm1_g, w_in, q_norm_g, k_norm_g, ssm_conv_w, ssm_conv_b, dt_bias, a_log,
           d_skip, ssm_norm_g, w_attn_o, w_ssm_o, w_out, norm2_g, w_up, ffn_conv_w, ffn_conv_b, w_down, attn_norm_2,
           w_in_2, b_forget_2, q_gain_2, k_gain_2, out_gain_2, w_out_2, mlp_norm_2, w_up_2, w_down_2):
    import concourse.bacc as bacc
    from concourse.bass_utils import run_bass_kernel_spmd

    def tiles(a):
        return np.asarray(a).reshape(-1, P).T

    def rows(a):
        return np.tile(np.asarray(a).reshape(1, -1), (P, 1))

    consts, alibi = shape_constants()
    params = np.stack([np.concatenate([
        tiles(norm1_g[l]), tiles(norm2_g[l]), tiles(ssm_norm_g[l]), tiles(ssm_conv_b[l]), tiles(ssm_conv_w[l]),
        tiles(ffn_conv_b[l]), tiles(ffn_conv_w[l]), tiles(np.repeat(np.asarray(d_skip[l]), HD)), rows(dt_bias[l]),
        rows(a_log[l]), rows(q_norm_g[l]), rows(k_norm_g[l])], axis=1) for l in range(DEPTH)])
    ada = np.stack([np.asarray(w_ada[l]).reshape(KT, P, 48, P).transpose(2, 1, 0, 3).reshape(48, P, KT * P)
                    for l in range(DEPTH)]).reshape(DEPTH * 48, P, KT * P)
    arrays = {
        "x_t": np.asarray(x)[0].T,
        "c_col": tiles(c),
        "pos": np.asarray(positions).reshape(TT, P).T,
        "consts": consts,
        "alibi": alibi,
        "params": params,
        "b_ada": np.concatenate([tiles(b_ada[l]) for l in range(DEPTH)], axis=1),
        "params2": np.concatenate([tiles(attn_norm_2[0]), tiles(mlp_norm_2[0]), rows(b_forget_2[0])], axis=1),
        "rows2": np.stack([rows(q_gain_2[0]), rows(k_gain_2[0]), rows(out_gain_2[0])], axis=1),
        "w_ada": ada,
        "stream": stream_of(*(np.asarray(a) for a in (w_in, w_attn_o, w_ssm_o, w_out, w_up, w_down,
                                                      w_in_2, w_out_2, w_up_2, w_down_2))),
    }
    nc = bacc.Bacc("TRN2", target_bir_lowering=False, num_devices=1)
    args, ins = [], {}
    for name, a in arrays.items():
        ins[f"in_{name}"] = np.ascontiguousarray(a)
        args.append(nc.dram_tensor(f"in_{name}", a.shape, mybir.dt.from_np(a.dtype), kind="ExternalInput").ap())
    out = nc.dram_tensor("out_x", (D, SEQ), mybir.dt.float32, kind="ExternalOutput").ap()
    build(nc, *args, out)
    r = run_bass_kernel_spmd(nc, [ins], core_ids=[0])
    return np.ascontiguousarray(r.results[0]["out_x"].T)[None]
```

```python
import math
from contextlib import ExitStack

import numpy as np
import concourse.bass as bass
from concourse import mybir

ds = bass.ds

P = 128
SEQ, D, DEPTH = 256, 1024, 2
TT = SEQ // P
KT = D // P
HEADS, HD = 16, 64
IDX_HEADS = 8
IDX_SCALE = (IDX_HEADS ** -0.5) * (HD ** -0.5)
KEEP = min(256, SEQ // 4)
TOP8 = KEEP // 8
D_INNER = 2 * D
SSM_HEADS, SSM_GROUPS, D_STATE = D_INNER // HD, 4, 128
XBC_TILES = (D_INNER + 2 * SSM_GROUPS * D_STATE) // P
SSM_CONV, FFN_CONV = 4, 3
D_FF, D_FF2 = 2816, 4096
FT, FT2 = D_FF // P, D_FF2 // P
N_MOBA, N_FOX, N_DIL = 4, 6, 6
G_COLS = N_FOX + N_FOX * HD
EPS = 1e-6
SCALE = HD ** -0.5
NEG = -1e30
PICKED = -3e38
CW = 3 * P

U_IDX, U_Q, U_KV, U_XBC, U_Z = 0, 4, 8, 16, 28
U_GA, U_AO, U_GM, U_SO, U_OUT, U_UP, U_DN = 36, 40, 44, 48, 56, 60, 82
DN_CHUNKS, DN2_CHUNKS = 6, 8
NCH = 2 * U_DN + 4 * DN_CHUNKS
NG = U_DN + 4
V_G, V_OUT, V_UP, V_DN = 12, 14, 18, 34
NCH2 = 2 * V_DN + 4 * DN2_CHUNKS
RING = 4
CHUNK = 4 * 256
SCAN_CHUNKS = (([], [[c] for c in range(16)], []),
               ([16, 17, 18, 19], [[20 + i] if i < 10 else [] for i in range(16)], [30, 31]))
N_ADA = DEPTH * 48


def chunk_words(l, c):
    if l < DEPTH:
        if c // 2 == 2:
            return 4 * 72
        if c // 2 == 3:
            return 4 * 32
        if c >= 2 * U_DN and (c - 2 * U_DN) % DN_CHUNKS == DN_CHUNKS - 1:
            return 2 * 256
    elif c // 2 == V_G + 1:
        return 4 * (G_COLS - 256)
    return CHUNK


def chunk_count(l):
    return NCH if l < DEPTH else NCH2


N_CHUNKS = DEPTH * NCH + NCH2
OFFSETS = [0]
for _g in range(N_CHUNKS):
    _l = min(_g // NCH, DEPTH)
    OFFSETS.append(OFFSETS[-1] + P * chunk_words(_l, _g - _l * NCH))

PRM_PARTS = [("norm1", KT), ("norm2", KT), ("ssmn", 16), ("convb", XBC_TILES), ("convw", 4 * XBC_TILES),
             ("ffnb", 2 * FT), ("ffnw", 3 * 2 * FT), ("skip", 16), ("dtb", 32), ("alog", 32), ("qg", HD), ("kg", HD)]
PRM = {}
_at = 0
for _n, _w in PRM_PARTS:
    PRM[_n] = (_at, _at + _w)
    _at += _w
PRM_W = _at
CONST_PARTS = [("ident", P), ("causal", CW), ("maskT", P), ("inv", HD // 2)]
CST = {}
_at = 0
for _n, _w in CONST_PARTS:
    CST[_n] = (_at, _at + _w)
    _at += _w
CST_W = _at
PRM2_W = 2 * KT + N_FOX


class Banks:

    def __init__(self, new_bank, new_sem, name, per_layer):
        self.bank = [new_bank(f"{name}_bank{b}") for b in range(2)]
        self.full = [new_sem(f"{name}_full{b}") for b in range(2)]
        self.read = [new_sem(f"{name}_read{b}") for b in range(2)]
        self.per_layer = per_layer

    def use(self, l, i):
        b = i % 2
        return b, l * ((self.per_layer + 1 - b) // 2) + i // 2


def build(nc, x_t, c_col, pos, consts, alibi, params, b_ada, params2, rows2, w_ada, stream, out):
    f32, f32r, bf16, i32 = mybir.dt.float32, mybir.dt.float32r, mybir.dt.bfloat16, mybir.dt.int32
    ALU, ACT, AX = mybir.AluOpType, mybir.ActivationFunctionType, mybir.AxisListType
    ctx = ExitStack()
    with ctx:
        def sb(name, shape, dt=f32):
            return ctx.enter_context(nc.sbuf_tensor(name, shape, dt))

        def sem(name):
            return ctx.enter_context(nc.semaphore(name))

        w_raw = sb("w_raw", [P, RING, CHUNK])
        w_hi = sb("w_hi", [P, RING, CHUNK], f32r)
        w_lo = sb("w_lo", [P, RING, CHUNK], f32r)
        XT = sb("residual", [P, KT, SEQ])
        ada_w = sb("ada_w", [P, 2, KT * P])
        CB = sb("c_dot_b", [P, SSM_GROUPS, CW])
        gated = sb("gated", [P, 2, 512])
        ada_acc = sb("ada_acc", [P, 4, P])
        cst = sb("consts_sb", [P, CST_W])
        prm = sb("params_sb", [P, PRM_W])
        prm2 = sb("params2_sb", [P, PRM2_W])
        bada = sb("b_ada_sb", [P, DEPTH * 48])
        mod = sb("mod", [P, DEPTH, 48])
        gain = sb("gain", [P, KT])
        ident_b = sb("ident_b", [P, P], bf16)
        maskT_b = sb("maskT_b", [P, P], bf16)
        ones = sb("ones", [P, SEQ])
        eps = sb("eps", [P, 1])
        c_act = sb("c_act", [P, KT])
        pos_i = sb("pos_i", [P, TT], i32)
        pos_f = sb("pos_f", [P, TT])
        sc_tab = sb("sin_cos", [P, 2, TT, 32])
        rt = sb("rope_tables", [P, 4, TT, 32])
        rs = sb("rstd_row", [P, 2, SEQ])
        probs = sb("probs", [P, 2, CW])
        probsT = sb("probsT", [P, 2, CW])
        keep_bias = sb("keep_bias", [P, CW])
        work = sb("work", [P, 4, 512])
        small = sb("small", [P, 256])
        root = sb("head_root", [P, 3, 32])
        neg_max = sb("neg_max", [P, HEADS, TT])
        row_max = sb("row_max", [P, HEADS, TT])
        row_sum = sb("row_sum", [P, HEADS, TT])
        row_inv = sb("row_inv", [P, HEADS, TT])
        iw = sb("idx_w", [P, TT, IDX_HEADS])
        dt_s = sb("dt", [P, TT, 32])
        neg_cs = sb("neg_cs", [P, TT, 32])
        a_row = sb("a_row", [32, SEQ])
        cs_row = sb("cs_row", [P, SEQ])
        conv = sb("conv", [P, 2, 512])

        def overlay(*sets):
            out, widest, top = [], 0, None
            for parts in sets:
                with ExitStack() as st:
                    row = []
                    total = 0
                    for name, shape, dt in parts:
                        row.append(st.enter_context(nc.sbuf_tensor(name, shape, dt)))
                        total += int(np.prod(shape[1:])) * 4
                    out.append(row)
                    if total > widest:
                        widest = total
            ctx.enter_context(nc.sbuf_tensor("region_" + sets[0][0][0], [P, widest // 4], f32))
            return out

        HH = sb("h_hi", [P, KT, SEQ], f32r)
        HL = sb("h_lo", [P, KT, SEQ], f32r)
        region = overlay(
            [("qkv", [P, 3, TT, D], f32),
             ("iq", [P, TT, 512], f32), ("iqT", [P, 4, SEQ], f32), ("ik", [P, TT, P], f32), ("ikT", [P, SEQ], f32),
             ("idx_relu", [P, 2, CW], f32), ("idx_score", [P, CW], f32), ("idx_left", [P, CW], f32),
             ("x_conv", [P, 16, SEQ], f32), ("bc_conv", [P, 8, SEQ], f32), ("z_gate", [P, 16, SEQ], f32)],
            [("sq", [P, KT, SEQ], f32), ("pad_a", [P, 16 * SEQ], f32), ("qT", [P, 8, SEQ], f32), ("kT", [P, 8, SEQ], f32)],
            [("gates", [P, 2, KT, SEQ], f32), ("x_dt", [P, TT, 1024], f32),
             ("oT_hi", [P, KT, SEQ], f32r), ("oT_lo", [P, KT, SEQ], f32r)],
            [("f_hi", [P, FT, SEQ], f32r), ("f_lo", [P, FT, SEQ], f32r)],
            [("f2_hi", [P, FT2, SEQ], f32r), ("f2_lo", [P, FT2, SEQ], f32r)],
            [("pad_c", [P, 40 * SEQ], f32), ("alibi_sb", [P, 10, CW], f32), ("fox_bias", [P, N_FOX, CW], f32),
             ("rows2_sb", [P, 3, D], f32), ("g2", [P, TT, G_COLS], f32)])
        (qkv, iq, iqT, ik, ikT, idx_relu, idx_score, idx_left, xs, bc, zg) = region[0]
        (sq, _, qT, kT), (gates, xdt, OTH, OTL), (FH, FL), (F2H, F2L), (_, alibi_sb, fox_bias, rows2_sb, g2) = region[1:]
        o_tok = qkv[:, 0]

        ident = cst[:, slice(*CST["ident"])]
        causal = cst[:, slice(*CST["causal"])]
        inv_freq = cst[:, slice(*CST["inv"])]

        def col(name, j, n=1):
            a = PRM[name][0] + j
            return prm[:, a:a + n]

        def bank(name):
            return ctx.enter_context(nc.psum_tensor(name, [P, 512], f32))

        gemm = [bank("gemm_bank0"), bank("gemm_bank1")]
        gemm_read = [sem("gemm_read0"), sem("gemm_read1")]
        S = Banks(bank, sem, "score", 60)
        T = Banks(bank, sem, "turn", 45)
        O = Banks(bank, sem, "outp", 22)
        mod_ps = S.bank[1][:, CW:CW + 2 * KT]
        mod_flat = mod[:].rearrange("p l c -> p (l c)")
        T_IQ, T_A, T_CS, T_QK, T_AT, T_OT, T_XDT, T_SUM = 0, 3, 4, 5, 13, 29, None, None
        S_IDX, S_AT, S_CB, S_SSM = 0, 8, 24, 28
        O_N1, O_AT, O_Y, O_N2 = 0, 1, 5, 21

        def t_half(hf):
            return 33 + 6 * hf, 33 + 6 * hf + 4
        T2_A, T2_QK, T2_AT, T2_OT = 0, 1, 9, 25
        S2_FOX, S2_AT = 0, 6
        O2_N1, O2_AT, O2_N2 = 0, 1, 5

        raw_full = [sem(f"raw_full{s}") for s in range(RING)]
        hi_ready, lo_ready, chunk_done = sem("hi_ready"), sem("lo_ready"), sem("chunk_done")
        ada_full = [sem("ada_full0"), sem("ada_full1")]
        ada_used, ada_summed, c_silu, z_ready = sem("ada_used"), sem("ada_summed"), sem("c_silu"), sem("z_ready")
        in_full, prm_full, tab_full, out_full = sem("in_full"), sem("prm_full"), sem("tab_full"), sem("out_full")
        set_up, c_ready, sin_arg, sin_done = sem("set_up"), sem("c_ready"), sem("sin_arg"), sem("sin_done")
        sq_ready, x_root, h_scaled, h_hi_ready, h_ready = (
            sem("sq_ready"), sem("x_root"), sem("h_scaled"), sem("h_hi_ready"), sem("h_ready"))
        idx_rot, relu_used = sem("idx_rot"), sem("relu_used")
        qk_sum, qk_root, qk_rot = sem("qk_sum"), sem("qk_root"), sem("qk_rot")
        sp_in, sp_exp, a_ready, cs_ready, ncs_ready = sem("sp_in"), sem("sp_exp"), sem("a_ready"), sem("cs_ready"), sem("ncs_ready")
        conv_first, conv_act = sem("conv_first"), sem("conv_act")
        max_ready, exp_done, o_ready, o_full = sem("max_ready"), sem("exp_done"), sem("o_ready"), sem("o_full")
        oT_hi_ready, oT_ready = sem("oT_hi_ready"), sem("oT_ready")
        g_ready, y_done = sem("g_ready"), sem("y_done")
        y_gated, y_sq, y_root, y_scaled, y_hi, y_ready = (
            sem("y_gated"), sem("y_sq"), sem("y_root"), sem("y_scaled"), sem("y_hi"), sem("y_ready"))
        mix_ready, mix_hi, mix_low = sem("mix_ready"), sem("mix_hi"), sem("mix_low")
        up_first, up_silu, up_prod, up_hi, up_ready = (
            sem("up_first"), sem("up_silu"), sem("up_prod"), sem("up_hi"), sem("up_ready"))
        og_in, og_root, sig_done = sem("og_in"), sem("og_root"), sem("sig_done")

        block = ctx.enter_context(nc.Block())

        def first_chunk(l, u):
            return l * NCH + 2 * u

        def unit_end(l, u):
            return l * NCH + 2 * u + 2

        def gemm_use(l, o):
            return o % 2, l * (NG // 2) + o // 2

        def ada_attention(l, h):
            return 48 * l + 2 * KT + h

        def ada_scan(l, f):
            return 48 * l + 4 * KT + f

        def ada_down(l, i):
            return 48 * (l + 1) + i

        def scan_unit(c):
            return U_GA + c // 2, c % 2

        @block.sync
        def _(sp):
            def load_chunk(g):
                l = min(g // NCH, DEPTH)
                n = chunk_words(l, g - l * NCH)
                if g >= RING:
                    sp.wait_ge(lo_ready, g - RING + 1)
                src = stream[OFFSETS[g]:OFFSETS[g + 1]].rearrange("(p n) -> p n", p=P)
                sp.dma_start(w_raw[:, g % RING, 0:n], src).then_inc(raw_full[g % RING], 16)

            def load_ada(a):
                if a >= 2:
                    sp.wait_ge(ada_used, a - 1)
                sp.dma_start(ada_w[:, a % 2, :], w_ada[a]).then_inc(ada_full[a % 2], 16)

            sp.dma_start(c_act[:], c_col).then_inc(in_full, 16)
            sp.dma_start(cst[:], consts).then_inc(in_full, 16)
            sp.dma_start(pos_i[:], pos).then_inc(in_full, 16)
            sp.dma_start(prm[:], params[0]).then_inc(prm_full, 16)
            sp.dma_start(bada[:], b_ada).then_inc(in_full, 16)
            sp.dma_start(prm2[:], params2).then_inc(in_full, 16)
            load_ada(0)
            load_ada(1)
            sp.dma_start(XT[:], x_t.rearrange("(k p) t -> p k t", p=P)).then_inc(in_full, 16)
            for a in range(2, 2 * KT):
                load_ada(a)
            for g in range(N_CHUNKS):
                l = min(g // NCH, DEPTH)
                c = g - l * NCH
                load_chunk(g)
                for la in range(DEPTH):
                    for h in range(HEADS):
                        if g == la * NCH + 2 * U_Z + 5 + h:
                            load_ada(ada_attention(la, h))
                    for f in range(16):
                        if g == la * NCH + 2 * U_GA + (5 + 2 * f if f < 8 else min(9 + 2 * f, 37)):
                            load_ada(ada_scan(la, f))
                    for i in range(16):
                        if la + 1 < DEPTH and g == la * NCH + 2 * U_DN + DN_CHUNKS * (i // 4) + i % 4 + 5:
                            load_ada(ada_down(la, i))
                if l < DEPTH and c == NCH - 1:
                    for b in range(2):
                        sp.wait_ge(gemm_read[b], gemm_use(l, U_DN - 2 + b)[1] + 1)
                    sp.wait_ge(up_first, (l + 1) * FT)
                    if l + 1 < DEPTH:
                        sp.dma_start(prm[:], params[l + 1]).then_inc(prm_full, 16)
                if l == DEPTH and c == 7:
                    sp.wait_ge(chunk_done, DEPTH * NCH)
                    sp.dma_start(alibi_sb[:], alibi).then_inc(tab_full, 16)
                    sp.dma_start(rows2_sb[:], rows2).then_inc(tab_full, 16)
            o3 = out.rearrange("(k p) t -> p k t", p=P)
            for j in range(4):
                b, k = gemm_use(DEPTH, V_DN + j)
                sp.wait_ge(gemm_read[b], k + 1)
                sp.dma_start(o3[:, 2 * j:2 * j + 2, :], XT[:, 2 * j:2 * j + 2, :]).then_inc(out_full, 16)
            sp.wait_ge(out_full, 64)

        @block.gpsimd
        def _(pool):
            for g in range(N_CHUNKS):
                l = min(g // NCH, DEPTH)
                n = chunk_words(l, g - l * NCH)
                s = g % RING
                pool.wait_ge(hi_ready, g + 1)
                if g >= RING:
                    pool.wait_ge(chunk_done, g - RING + 1)
                nc.gpsimd.tensor_tensor(w_lo[:, s, 0:n], w_raw[:, s, 0:n], w_hi[:, s, 0:n].bitcast(f32),
                                        ALU.subtract).then_inc(lo_ready, 1)

        @block.scalar
        def _(act):
            A = nc.scalar.activation

            def high(g):
                if g >= N_CHUNKS:
                    return
                l = min(g // NCH, DEPTH)
                n = chunk_words(l, g - l * NCH)
                s = g % RING
                act.wait_ge(raw_full[s], 16 * (g // RING + 1))
                if g >= RING:
                    act.wait_ge(chunk_done, g - RING + 1)
                A(w_hi[:, s, 0:n], w_raw[:, s, 0:n], ACT.Copy).then_inc(hi_ready, 1)

            def scan_chunk(l, c):
                u, second = scan_unit(c)
                high(first_chunk(l, u) + second + RING)
                if second and (U_GA <= u < U_AO or U_GM <= u < U_SO):
                    act.wait_ge(chunk_done, unit_end(l, u))
                    j = 2 * (u % 4)
                    A(gates[:, 0 if u < U_AO else 1, j:j + 2, :], gemm[u % 2][:], ACT.Tanh, scale=0.5).then_inc(gemm_read[u % 2], 1)

            def after_unit(l, u):
                for g in range(first_chunk(l, u), first_chunk(l, u) + 2):
                    high(g + RING)
                act.wait_ge(chunk_done, unit_end(l, u))

            def norm(l, which, bias, summed):
                for j in range(4):
                    if summed:
                        b, k = gemm_use(summed[0], summed[1] + j)
                        act.wait_ge(gemm_read[b], k + 1)
                    A(sq[:, 2 * j:2 * j + 2, :], XT[:, 2 * j:2 * j + 2, :], ACT.Square).then_inc(sq_ready, 1)
                n = 2 * l + which
                i = (O_N2 if which else O_N1) if l < DEPTH else (O2_N2 if which else O2_N1)
                b, k = O.use(l, i)
                act.wait_ge(O.read[b], k + 1)
                A(rs[:, 0, :], rs[:, 1, :], ACT.Sqrt).then_inc(x_root, 1)
                for kt in range(KT):
                    act.wait_ge(h_scaled, n * KT + kt + 1)
                    if bias is None:
                        A(HH[:, kt, :], sq[:, kt, :], ACT.Copy).then_inc(h_hi_ready, 1)
                    else:
                        A(HH[:, kt, :], sq[:, kt, :], ACT.Identity, bias=bias[:, kt:kt + 1]).then_inc(h_hi_ready, 1)

            def attention(l):
                s0, t0 = (S_AT, T_AT) if l < DEPTH else (S2_AT, T2_AT)
                for h in range(HEADS):
                    b = h % 2
                    act.wait_ge(max_ready, l * HEADS + h + 1)
                    A(probs[:, b, 0:P], probs[:, b, 0:P], ACT.Exp, scale=SCALE, bias=neg_max[:, h, 0:1],
                      accum_out=row_sum[:, h, 0:1])
                    A(probs[:, b, P:CW], probs[:, b, P:CW], ACT.Exp, scale=SCALE, bias=neg_max[:, h, 1:2],
                      accum_out=row_sum[:, h, 1:2]).then_inc(exp_done, 1)
                    if h >= 1 and (h - 1) % 2 == 0:
                        turn_evac(l, h - 1, t0)
                    if l < DEPTH and h:
                        z_chunk(l, h - 1)
                if l < DEPTH:
                    z_chunk(l, HEADS - 1)

            def z_chunk(l, c):
                u = U_Z + c // 2
                high(first_chunk(l, U_Z) + c + RING)
                if c % 2:
                    act.wait_ge(chunk_done, unit_end(l, u))
                    A(zg[:, c - 1:c + 1, :], gemm[u % 2][:], ACT.Copy).then_inc(gemm_read[u % 2], 1)

            def turn_evac(l, h, t0):
                b, k = T.use(l, t0 + h)
                act.wait_ge(T.full[b], k + 1)
                A(probsT[:, h % 2, :], T.bank[b][:, 0:CW], ACT.Copy).then_inc(T.read[b], 1)

            def turn_qk(l, t0):
                for r in range(0, 8, 2):
                    b, k = T.use(l, t0 + r)
                    act.wait_ge(T.full[b], k + 1)
                    dst = qT if r < 4 else kT
                    j = 2 * (r % 4)
                    A(dst[:, j:j + 2, :], T.bank[b][:], ACT.Copy).then_inc(T.read[b], 1)

            def square_y(l, f):
                act.wait_ge(y_gated, l * 16 + f + 1)
                if f % 4 == 0 and f:
                    hf, gi = (f // 4 - 1) // 2, (f // 4 - 1) % 2
                    b, k = T.use(l, t_half(hf)[1] + gi)
                    act.wait_ge(T.full[b], k + 1)
                A(work[:, f % 4, SEQ:2 * SEQ], zg[:, f, :], ACT.Square).then_inc(y_sq, 1)

            def turn_o(l, t0):
                for r in range(4):
                    b, k = T.use(l, t0 + r)
                    act.wait_ge(T.full[b], k + 1)
                    A(OTH[:, 2 * r:2 * r + 2, :], T.bank[b][:], ACT.Copy).then_inc(oT_hi_ready, 1)

            act.wait_ge(in_full, 96)
            A(small[:, 0:KT], c_act[:], ACT.Tanh, scale=0.5).then_inc(c_ready, 1)
            act.wait_ge(sin_arg, 1)
            A(sc_tab[:], sc_tab[:], ACT.Sin).then_inc(sin_done, 1)
            for g in range(RING):
                high(g)

            for l in range(DEPTH):
                act.wait_ge(set_up, 1)
                norm(l, 0, mod[:, l, 0:KT], (l - 1, U_DN) if l else None)
                for u in range(U_IDX, U_Q):
                    after_unit(l, u)
                act.wait_ge(sp_in, l + 1)
                A(small[:, 0:64], small[:, 0:64], ACT.Exp).then_inc(sp_exp, 1)
                A(small[:, 128:160], prm[:, slice(*PRM["alog"])], ACT.Exp).then_inc(sp_exp, 1)
                for u in range(U_Q, U_XBC):
                    if u == U_Q + 2:
                        for h in range(IDX_HEADS):
                            b, k = S.use(l, S_IDX + h)
                            act.wait_ge(S.full[b], k + 1)
                            if h >= 2:
                                act.wait_ge(relu_used, l * IDX_HEADS + h - 1)
                            A(idx_relu[:, h % 2, :], S.bank[b][:, 0:CW], ACT.Relu).then_inc(S.read[b], 1)
                    if u in (U_KV + 2, U_KV + 7):
                        i = (u - U_KV) // 4
                        act.wait_ge(qk_sum, 2 * l + i + 1)
                        A(root[:, i, :], small[:, 64 + 32 * i:96 + 32 * i], ACT.Sqrt).then_inc(qk_root, 1)
                    after_unit(l, u)
                    i, j = (u - U_Q) // 4, (u - U_Q) % 4
                    A(qkv[:, i, :, 256 * j:256 * j + 256], gemm[u % 2][:].rearrange("p (t n) -> p t n", t=TT),
                      ACT.Copy).then_inc(gemm_read[u % 2], 1)

                def conv_silu(v):
                    b, k = gemm_use(l, U_XBC + v)
                    act.wait_ge(gemm_read[b], k + 1)
                    dst = xs[:, 2 * v:2 * v + 2, :] if v < 8 else bc[:, 2 * v - 16:2 * v - 14, :]
                    A(dst, conv[:, v % 2, :], ACT.Silu).then_inc(conv_act, 1)

                for u in range(U_XBC, U_Z):
                    after_unit(l, u)
                    v = u - U_XBC
                    if v >= 2:
                        act.wait_ge(conv_act, l * 12 + v - 1)
                    for j in range(2):
                        t = 2 * v + j
                        A(conv[:, v % 2, j * SEQ:(j + 1) * SEQ], gemm[u % 2][:, j * SEQ:(j + 1) * SEQ], ACT.Identity,
                          scale=col("convw", 3 * XBC_TILES + t), bias=col("convb", t)).then_inc(conv_first, 1)
                    if v:
                        conv_silu(v - 1)
                conv_silu(11)
                turn_qk(l, T_QK)
                attention(l)
                for b in range(2):
                    act.wait_ge(gemm_read[b], gemm_use(l, U_GA - 2 + b)[1] + 1)
                for j in range(0, 16, 2):
                    A(zg[:, j:j + 2, :], zg[:, j:j + 2, :], ACT.Silu).then_inc(z_ready, 1)
                turn_o(l, T_OT)
                for hf in range(2):
                    tx, ts = t_half(hf)
                    before, at_head, after = SCAN_CHUNKS[hf]
                    for c in before:
                        scan_chunk(l, c)
                    for h in range(16 * hf, 16 * hf + 16):
                        b, k = S.use(l, S_SSM + h)
                        act.wait_ge(S.full[b], k + 1)
                        n = l * 32 + h
                        if n >= 2:
                            act.wait_ge(g_ready, n - 1)
                        if h == 0:
                            act.wait_ge(ncs_ready, l + 1)
                        A(probs[:, b, 0:2 * P], S.bank[b][:, 0:2 * P], ACT.Exp, bias=neg_cs[:, 0, h:h + 1])
                        A(probs[:, b, 2 * P:CW], S.bank[b][:, 2 * P:CW], ACT.Exp, bias=neg_cs[:, 1, h:h + 1]
                          ).then_inc(S.read[b], 1)
                        if h % 16:
                            for c in at_head[h % 16 - 1]:
                                scan_chunk(l, c)
                        if h % 2 and h > 16 * hf + 1:
                            square_y(l, h // 2 - 1)
                    for c in at_head[15]:
                        scan_chunk(l, c)
                    square_y(l, 8 * hf + 7)
                    for c in after:
                        scan_chunk(l, c)
                    for gi in range(2):
                        b, k = T.use(l, ts + gi)
                        act.wait_ge(T.read[b], k + 1)
                        A(rs[:, gi, :], work[:, gi, 0:SEQ], ACT.Sqrt).then_inc(y_root, 1)
                    for f in range(8):
                        n = l * 16 + 8 * hf + f
                        act.wait_ge(y_scaled, n + 1)
                        if f == 0:
                            act.wait_ge(chunk_done, unit_end(l, U_SO + 3 if hf else U_AO + 3))
                        A(OTH[:, f, :], zg[:, 8 * hf + f, :], ACT.Copy).then_inc(y_hi, 1)
                for u in range(U_SO + 4, U_SO + 8):
                    after_unit(l, u)
                for j in range(4):
                    act.wait_ge(mix_ready, l * 4 + j + 1)
                    A(HH[:, 2 * j:2 * j + 2, :], gates[:, 0, 2 * j:2 * j + 2, :], ACT.Copy, scale=0.5).then_inc(mix_hi, 1)
                for u in range(U_OUT, U_UP):
                    after_unit(l, u)
                norm(l, 1, mod[:, l, 24:32], (l, U_OUT))
                def up_gate(i):
                    b, k = gemm_use(l, U_UP + i)
                    act.wait_ge(gemm_read[b], k + 1)
                    if i >= 4:
                        act.wait_ge(up_ready, l * FT + i - 3)
                    A(work[:, i % 4, 0:SEQ], conv[:, i % 2, SEQ:2 * SEQ], ACT.Silu).then_inc(up_silu, 1)

                def up_high(i):
                    act.wait_ge(up_prod, l * FT + i + 1)
                    A(FH[:, i, :], work[:, i % 4, 0:SEQ], ACT.Copy).then_inc(up_hi, 1)

                for u in range(U_UP, U_DN):
                    after_unit(l, u)
                    i = u - U_UP
                    n = l * FT + i
                    if i >= 2:
                        act.wait_ge(up_prod, n - 1)
                    for j in range(2):
                        t = j * FT + i
                        a = A(conv[:, i % 2, j * SEQ:(j + 1) * SEQ], gemm[u % 2][:, j * SEQ:(j + 1) * SEQ], ACT.Identity,
                              scale=col("ffnw", 2 * 2 * FT + t), bias=col("ffnb", t))
                    a.then_inc(up_first, 1)
                    if i >= 1:
                        up_gate(i - 1)
                    if i >= 2:
                        up_high(i - 2)
                up_gate(FT - 1)
                up_high(FT - 2)
                up_high(FT - 1)
                for g in range(l * NCH + 2 * U_DN, (l + 1) * NCH):
                    high(g + RING)

            l = DEPTH
            norm(l, 0, None, (l - 1, U_DN))
            for u in range(0, V_G + 2):
                after_unit(l, u)
                if u < V_G:
                    i, j = u // 4, u % 4
                    A(qkv[:, i, :, 256 * j:256 * j + 256], gemm[u % 2][:].rearrange("p (t n) -> p t n", t=TT),
                      ACT.Copy).then_inc(gemm_read[u % 2], 1)
                else:
                    a, n = (0, 256) if u == V_G else (256, G_COLS - 256)
                    A(g2[:, :, a:a + n], gemm[u % 2][:].rearrange("p (t n) -> p t n", t=TT)[:, :, 0:n],
                      ACT.Copy).then_inc(gemm_read[u % 2], 1)
                if u == 8 or u == 12:
                    i = u // 12
                    act.wait_ge(qk_sum, 2 * l + i + 1)
                    A(root[:, i, :], small[:, 64 + 32 * i:96 + 32 * i], ACT.Sqrt).then_inc(qk_root, 1)
            act.wait_ge(sp_in, l + 1)
            A(small[:, 0:2 * N_FOX], small[:, 0:2 * N_FOX], ACT.Exp).then_inc(sp_exp, 1)
            turn_qk(l, T2_QK)
            attention(l)
            A(g2[:, :, N_FOX:], g2[:, :, N_FOX:], ACT.Sigmoid).then_inc(sig_done, 1)
            act.wait_ge(og_in, 1)
            A(root[:, 2, 0:6], small[:, 0:6], ACT.Sqrt).then_inc(og_root, 1)
            turn_o(l, T2_OT)
            for u in range(V_OUT, V_UP):
                after_unit(l, u)
            norm(l, 1, None, (l, V_OUT))
            def up2_high(i):
                b, k = gemm_use(l, V_UP + i)
                act.wait_ge(gemm_read[b], k + 1)
                A(F2H[:, 2 * i:2 * i + 2, :], work[:, i % 4, :], ACT.Copy).then_inc(up_hi, 1)

            for u in range(V_UP, V_DN):
                after_unit(l, u)
                i = u - V_UP
                if i >= 2:
                    b, k = gemm_use(l, u - 2)
                    act.wait_ge(gemm_read[b], k + 1)
                A(conv[:, i % 2, :], gemm[u % 2][:], ACT.Relu).then_inc(up_first, 1)
                if i >= 1:
                    up2_high(i - 1)
            up2_high(V_DN - V_UP - 1)
            for g in range(l * NCH + 2 * V_DN, N_CHUNKS - RING):
                high(g + RING)

        @block.vector
        def _(dve):
            V = nc.vector

            def stt(out, in0, scalar, in1, op0, op1):
                return V.scalar_tensor_tensor(out=out, in0=in0, scalar=scalar, in1=in1, op0=op0, op1=op1)

            def mods(a, n, ps):
                V.tensor_tensor(mod_flat[:, a:a + n], ps, bada[:, a:a + n], ALU.add)

            def ada(a):
                dve.wait_ge(ada_full[a % 2], 16 * (a // 2 + 1))
                w = ada_w[:, a % 2, :].rearrange("p (k n) -> p k n", k=KT)
                V.tensor_tensor(w, w, c_act[:].unsqueeze(2).to_broadcast([P, KT, P]), ALU.mult)
                if a >= 2 * KT + 4:
                    dve.wait_ge(ada_summed, a - 2 * KT - 3)
                dve.drain()
                V.tensor_reduce(out=ada_acc[:, a % 4, :], in_=ada_w[:, a % 2, :].rearrange("p (k n) -> p n k", k=KT),
                                axis=AX.X, op=ALU.add).then_inc(ada_used, 1)

            def rsqrt(r, v, w):
                V.reciprocal(r, r)
                dve.drain()
                V.tensor_tensor(w, r, r, ALU.mult)
                dve.drain()
                V.tensor_tensor(w, w, v, ALU.mult)
                dve.drain()
                V.tensor_scalar(w, w, -0.5, 1.5, ALU.mult, ALU.add)
                dve.drain()
                ins = V.tensor_tensor(r, r, w, ALU.mult)
                dve.drain()
                return ins

            def norm(l, which, g_col, scale_col, shift):
                n = 2 * l + which
                if scale_col is None:
                    V.tensor_copy(gain[:], g_col)
                else:
                    stt(gain[:], scale_col, 1.0, g_col, ALU.add, ALU.mult)
                i = (O_N2 if which else O_N1) if l < DEPTH else (O2_N2 if which else O2_N1)
                b, k = O.use(l, i)
                dve.wait_ge(o_full, 6 * l + (6 if which else 1))
                if l < DEPTH and which:
                    mods(ada_scan(l, 15), 1, O.bank[b][:, SEQ:SEQ + 1])
                V.tensor_scalar(rs[:, 1, :], O.bank[b][:, 0:SEQ], 1.0 / D, EPS, ALU.mult, ALU.add).then_inc(O.read[b], 1)
                dve.wait_ge(x_root, n + 1)
                dve.drain()
                rsqrt(rs[:, 0, :], rs[:, 1, :], work[:, 0, 0:SEQ])
                for kt in range(KT):
                    stt(sq[:, kt, :], XT[:, kt, :], gain[:, kt:kt + 1], rs[:, 0, :], ALU.mult, ALU.mult).then_inc(h_scaled, 1)
                for kt in range(KT):
                    dve.wait_ge(h_hi_ready, n * KT + kt + 1)
                    if shift is None:
                        V.tensor_tensor(HL[:, kt, :], sq[:, kt, :], HH[:, kt, :].bitcast(f32), ALU.subtract).then_inc(h_ready, 1)
                    else:
                        stt(HL[:, kt, :], sq[:, kt, :], shift[:, kt:kt + 1], HH[:, kt, :].bitcast(f32),
                            ALU.add, ALU.subtract).then_inc(h_ready, 1)

            def bc3(ap, n, m):
                return ap.unsqueeze(1).to_broadcast([P, m, n])

            def rope(x, heads, tab, tt):
                n = heads * 32
                w = [work[:, i, 0:n].rearrange("p (h e) -> p h e", e=32) for i in range(3)]
                x1, x2 = x[:, :, 0:32], x[:, :, 32:64]
                t = [bc3(tab[i][:, tt, :], 32, heads) for i in range(4)]
                dve.drain()
                V.tensor_tensor(w[0], x1, t[0], ALU.mult)
                V.tensor_tensor(w[1], x2, t[1], ALU.mult)
                V.tensor_tensor(w[2], x2, t[2], ALU.mult)
                dve.drain()
                V.tensor_tensor(x2, x1, t[3], ALU.mult)
                dve.drain()
                V.tensor_tensor(x1, w[0], w[1], ALU.subtract)
                return V.tensor_tensor(x2, w[2], x2, ALU.add)

            def qk_norm(l, i, g_row):
                r = small[:, 64 + 32 * i:96 + 32 * i]
                for tt in range(TT):
                    x = qkv[:, i, tt, :]
                    for hf in range(2):
                        dve.drain()
                        V.tensor_tensor(work[:, hf, :], x[:, 512 * hf:512 * hf + 512], x[:, 512 * hf:512 * hf + 512], ALU.mult)
                        dve.drain()
                        V.tensor_reduce(out=r[:, 16 * tt + 8 * hf:16 * tt + 8 * hf + 8],
                                        in_=work[:, hf, :].rearrange("p (h e) -> p h e", e=HD), axis=AX.X, op=ALU.add)
                dve.drain()
                V.tensor_scalar(r, r, 1.0 / HD, EPS, ALU.mult, ALU.add).then_inc(qk_sum, 1)
                dve.wait_ge(qk_root, 2 * l + i + 1)
                r, v = root[:, i, :], r
                rsqrt(r, v, work[:, 0, 0:32])
                for tt in range(TT):
                    x = qkv[:, i, tt, :].rearrange("p (h e) -> p h e", e=HD)
                    a = V.tensor_tensor(x, x, r[:, 16 * tt:16 * tt + 16].unsqueeze(2).to_broadcast([P, HEADS, HD]), ALU.mult)
                return a

            def tables(g0):
                g1, g2_ = prm[:, g0:g0 + 32], prm[:, g0 + 32:g0 + 64]
                sn, cs = sc_tab[:, 0], sc_tab[:, 1]
                dve.drain()
                for i, (t, g) in enumerate(((cs, g1), (sn, g2_), (cs, g2_), (sn, g1))):
                    V.tensor_tensor(rt[:, i], t, bc3(g, 32, TT), ALU.mult)

            def softplus(x, u, n, sign):
                z, z2, s = small[:, 160:160 + n], work[:, 3, 0:n], work[:, 3, 64:64 + n]
                V.tensor_scalar(z2, u, 2.0, None, ALU.add)
                dve.drain()
                V.reciprocal(z2, z2)
                dve.drain()
                V.tensor_tensor(z, u, z2, ALU.mult)
                dve.drain()
                V.tensor_tensor(z2, z, z, ALU.mult)
                dve.drain()
                V.tensor_scalar(s, z2, 1.0 / 17, None, ALU.mult)
                for d in (15, 13, 11, 9, 7, 5, 3):
                    dve.drain()
                    stt(s, s, 1.0 / d, z2, ALU.add, ALU.mult)
                dve.drain()
                stt(s, s, 1.0, z, ALU.add, ALU.mult)
                V.tensor_scalar(x, x, 0.0, None, ALU.max)
                dve.drain()
                stt(x, s, 2.0, x, ALU.mult, ALU.add)
                dve.drain()
                if sign < 0:
                    V.tensor_scalar(x, x, -1.0, None, ALU.mult)
                    dve.drain()

            def turn_qk(l, t0):
                for r in range(1, 8, 2):
                    b, k = T.use(l, t0 + r)
                    dve.wait_ge(T.full[b], k + 1)
                    dst = qT if r < 4 else kT
                    j = 2 * (r % 4)
                    V.tensor_copy(dst[:, j:j + 2, :], T.bank[b][:]).then_inc(T.read[b], 1)

            def attention(l, bias_of):
                s0, t0, o0 = (S_AT, T_AT, O_AT) if l < DEPTH else (S2_AT, T2_AT, O2_AT)

                def turn_evac(h):
                    b, k = T.use(l, t0 + h)
                    dve.wait_ge(T.full[b], k + 1)
                    V.tensor_copy(probsT[:, h % 2, :], T.bank[b][:, 0:CW]).then_inc(T.read[b], 1)

                def normalise(q4):
                    b, k = O.use(l, o0 + q4)
                    dve.wait_ge(o_full, 6 * l + 2 + q4)
                    h0 = 4 * q4
                    V.reciprocal(row_inv[:, h0:h0 + 4, :], row_sum[:, h0:h0 + 4, :])
                    dve.drain()
                    for tt in range(TT):
                        o = O.bank[b][:].rearrange("p (h t d) -> p h t d", h=4, t=TT)[:, :, tt, :]
                        ins = V.tensor_tensor(o_tok[:, tt, 64 * h0:64 * h0 + 256].rearrange("p (h d) -> p h d", d=HD), o,
                                              row_inv[:, h0:h0 + 4, tt].unsqueeze(2).to_broadcast([P, 4, HD]), ALU.mult)
                    ins.then_inc(O.read[b], 1)

                for h in range(HEADS):
                    b, k = S.use(l, s0 + h)
                    dve.wait_ge(S.full[b], k + 1)
                    if h >= 2:
                        b2, k2 = T.use(l, t0 + h - 2)
                        dve.wait_ge(T.full[b2], k2 + 1)
                    bias = bias_of(h)
                    dve.drain()
                    if l < DEPTH and h % 2 and h > 1:
                        mods(ada_attention(l, h - 3), 2, S.bank[b][:, CW:CW + 2])
                    for a, e, tt in ((0, P, 0), (P, CW, 1)):
                        ins = V.tensor_tensor_reduce(out=probs[:, h % 2, a:e], in0=S.bank[b][:, a:e], in1=bias[:, a:e], scale=1.0,
                                                     scalar=PICKED, op0=ALU.add, op1=ALU.max, accum_out=row_max[:, h, tt:tt + 1])
                    ins.then_inc(S.read[b], 1)
                    dve.drain()
                    V.tensor_scalar(neg_max[:, h, :], row_max[:, h, :], -SCALE, None, ALU.mult).then_inc(max_ready, 1)
                    if h >= 1 and (h - 1) % 2:
                        turn_evac(h - 1)
                    if h % 4 == 2 and h > 2:
                        normalise(h // 4 - 1)
                    if l < DEPTH:
                        ada(ada_attention(l, h))
                turn_evac(HEADS - 1)
                normalise(3)

            def turn_o(l, t0):
                for r in range(4):
                    b, k = T.use(l, t0 + r)
                    dve.wait_ge(oT_hi_ready, l * 4 + r + 1)
                    V.tensor_tensor(OTL[:, 2 * r:2 * r + 2, :], T.bank[b][:].rearrange("p (k t) -> p k t", k=2),
                                    OTH[:, 2 * r:2 * r + 2, :].bitcast(f32), ALU.subtract).then_inc(T.read[b], 1)

            def add_to_x(l, o, j, g_col):
                b, k = gemm_use(l, o)
                for i in range(2):
                    g = 1.0 if g_col is None else g_col[:, 2 * j + i:2 * j + i + 1]
                    ins = stt(XT[:, 2 * j + i, :], gemm[b][:, i * SEQ:(i + 1) * SEQ], g, XT[:, 2 * j + i, :], ALU.mult, ALU.add)
                ins.then_inc(gemm_read[b], 1)

            V.memset(ones[:], 1.0)
            V.memset(eps[:], EPS)
            V.memset(cs_row[:], 0.0)
            dve.wait_ge(in_full, 96)
            V.tensor_copy(ident_b[:], ident)
            V.tensor_copy(maskT_b[:], cst[:, slice(*CST["maskT"])]).then_inc(set_up, 1)
            dve.wait_ge(c_ready, 1)
            stt(small[:, 0:KT], small[:, 0:KT], 1.0, c_act[:], ALU.add, ALU.mult)
            dve.drain()
            V.tensor_scalar(c_act[:], small[:, 0:KT], 0.5, None, ALU.mult).then_inc(c_silu, 1)
            V.tensor_copy(pos_f[:], pos_i[:])
            dve.drain()
            two_pi = (6.28125, float(np.float32(2 * math.pi - 6.28125)), float(2 * math.pi - 6.28125 - float(np.float32(2 * math.pi - 6.28125))))
            ang, turns = work[:, 0, 0:64], work[:, 1, 0:64]
            for tt in range(TT):
                V.tensor_scalar(ang[:, 32 * tt:32 * tt + 32], inv_freq, pos_f[:, tt:tt + 1], None, ALU.mult)
            magic = 1.5 * 2.0 ** 23
            for i, shift in ((0, 0.0), (1, 0.25)):
                r = sc_tab[:, i].rearrange("p t e -> p (t e)")
                dve.drain()
                V.tensor_scalar(turns, ang, 1.0 / (2 * math.pi), shift, ALU.mult, ALU.add)
                dve.drain()
                V.tensor_scalar(turns, turns, magic, None, ALU.add)
                dve.drain()
                V.tensor_scalar(turns, turns, magic, None, ALU.subtract)
                dve.drain()
                stt(r, turns, -two_pi[0], ang, ALU.mult, ALU.add)
                for part in two_pi[1:]:
                    dve.drain()
                    stt(r, turns, -part, r, ALU.mult, ALU.add)
                dve.drain()
                V.tensor_scalar(r, r, i * math.pi / 2, 3.1415925, ALU.add, ALU.min)
                dve.drain()
                V.tensor_scalar(r, r, -3.1415925, None, ALU.max)
            dve.drain().then_inc(sin_arg, 1)
            dve.wait_ge(ada_used, 2 * KT)
            mods(0, 2 * KT, mod_ps)

            for l in range(DEPTH):
                dve.wait_ge(prm_full, 16 * (l + 1))
                dve.drain()
                norm(l, 0, col("norm1", 0, KT), mod[:, l, 8:16], mod[:, l, 0:8])
                for u in range(U_IDX, U_Q):
                    b, k = gemm_use(l, u)
                    dve.wait_ge(chunk_done, unit_end(l, u))
                    src = gemm[b][:].rearrange("p (t n) -> p t n", t=TT)
                    if u < 2:
                        V.tensor_copy(iq[:, :, 256 * u:256 * u + 256], src).then_inc(gemm_read[b], 1)
                    elif u == 2:
                        V.tensor_copy(ik[:, :, 0:HD], src[:, :, 0:HD])
                        V.tensor_copy(iw[:], src[:, :, HD:HD + IDX_HEADS]).then_inc(gemm_read[b], 1)
                    else:
                        V.tensor_tensor(dt_s[:], src[:, :, 0:32], bc3(col("dtb", 0, 32), 32, TT), ALU.add).then_inc(gemm_read[b], 1)
                dve.drain()
                d2 = dt_s[:].rearrange("p t h -> p (t h)")
                stt(small[:, 0:64], d2, -1.0, d2, ALU.mult, ALU.min).then_inc(sp_in, 1)
                if l == 0:
                    dve.wait_ge(sin_done, 1)
                sn, cs = sc_tab[:, 0], sc_tab[:, 1]
                plain = (cs, sn, cs, sn)
                for tt in range(TT):
                    rope(ik[:, tt, 0:HD].rearrange("p (h e) -> p h e", e=HD), 1, plain, tt)
                dve.drain()
                V.tensor_copy(ik[:, :, HD:P], ik[:, :, 0:HD])
                for tt in range(TT):
                    ins = rope(iq[:, tt, :].rearrange("p (h e) -> p h e", e=HD), IDX_HEADS, plain, tt)
                dve.drain().then_inc(idx_rot, 1)
                dve.wait_ge(sp_exp, 2 * l + 2)
                softplus(d2, small[:, 0:64], 64, 1)
                V.scalar_tensor_tensor(out=small[:, 0:64].rearrange("p (t h) -> p t h", t=TT), in0=dt_s[:], scalar=-1.0,
                                       in1=bc3(small[:, 128:160], 32, TT), op0=ALU.mult, op1=ALU.mult).then_inc(a_ready, 1)
                for r in range(3):
                    b, k = T.use(l, T_IQ + r)
                    dve.wait_ge(T.full[b], k + 1)
                    dst = iqT[:, 2 * r:2 * r + 2, :] if r < 2 else ikT[:]
                    V.tensor_copy(dst, T.bank[b][:] if r < 2 else T.bank[b][:, 0:SEQ]).then_inc(T.read[b], 1)
                for h in range(IDX_HEADS):
                    b, k = S.use(l, S_IDX + h)
                    dve.wait_ge(S.read[b], k + 1)
                    for a, e, tt in ((0, P, 0), (P, CW, 1)):
                        if h == 0:
                            ins = V.tensor_scalar(idx_score[:, a:e], idx_relu[:, 0, a:e], iw[:, tt, 0:1], None, ALU.mult)
                        else:
                            ins = stt(idx_score[:, a:e], idx_relu[:, h % 2, a:e], iw[:, tt, h:h + 1], idx_score[:, a:e],
                                      ALU.mult, ALU.add)
                    ins.then_inc(relu_used, 1)
                    dve.drain()
                stt(idx_score[:], idx_score[:], IDX_SCALE, causal, ALU.mult, ALU.add)
                b, k = T.use(l, T_A)
                dve.wait_ge(T.full[b], k + 1)
                V.tensor_copy(a_row[:], T.bank[b][0:32, 0:SEQ]).then_inc(T.read[b], 1)
                dve.drain()
                V.tensor_tensor_scan(out=cs_row[0:32, :], data0=ones[0:32, :], data1=a_row[:], initial=0.0,
                                     op0=ALU.mult, op1=ALU.add).then_inc(cs_ready, 1)
                for i in range(TOP8):
                    src = idx_left if i else idx_score
                    dve.drain()
                    for a, e, tt in ((0, P, 0), (P, CW, 1)):
                        V.max(small[:, 224 + 8 * tt:232 + 8 * tt], src[:, a:e])
                    dve.drain()
                    for a, e, tt in ((0, P, 0), (P, CW, 1)):
                        V.match_replace(out=idx_left[:, a:e], in_to_replace=small[:, 224 + 8 * tt:232 + 8 * tt], in_values=src[:, a:e],
                                        imm_value=PICKED)
                dve.drain()
                V.tensor_scalar(keep_bias[:], idx_left[:], -2e38, NEG, ALU.is_gt, ALU.mult)
                dve.drain()
                V.tensor_tensor(keep_bias[:], keep_bias[:], causal, ALU.add)
                for i in range(2):
                    for b in range(2):
                        k = gemm_use(l, U_Q + 4 * i + 2 + b)[1]
                        dve.wait_ge(gemm_read[b], k + 1)
                    tables(PRM["qg"][0] if i == 0 else PRM["kg"][0])
                    qk_norm(l, i, None)
                    for tt in range(TT):
                        rope(qkv[:, i, tt, :].rearrange("p (h e) -> p h e", e=HD), HEADS, [rt[:, q] for q in range(4)], tt)
                    dve.drain().then_inc(qk_rot, 1)
                for u in range(U_XBC, U_Z):
                    v = u - U_XBC
                    b, k = gemm_use(l, u)
                    dve.wait_ge(conv_first, l * 24 + 2 * v + 2)
                    for d in range(1, SSM_CONV):
                        if d > 1:
                            dve.drain()
                        for j in range(2):
                            o = j * SEQ
                            c = conv[:, v % 2, o + d:o + SEQ]
                            ins = stt(c, gemm[b][:, o:o + SEQ - d], col("convw", (3 - d) * XBC_TILES + 2 * v + j), c, ALU.mult, ALU.add)
                    ins.then_inc(gemm_read[b], 1)
                    dve.drain()
                b, k = T.use(l, T_CS)
                dve.wait_ge(T.full[b], k + 1)
                V.tensor_scalar(neg_cs[:], T.bank[b][:, 0:64].rearrange("p (t h) -> p t h", t=TT), -1.0, None, ALU.mult
                                ).then_inc(T.read[b], 1)
                dve.drain().then_inc(ncs_ready, 1)
                turn_qk(l, T_QK)
                attention(l, lambda h: keep_bias)
                dve.drain().then_inc(o_ready, 1)

                def scan_chunk(c):
                    u, second = scan_unit(c)
                    j = 2 * (u % 4)
                    if not second or U_GM <= u < U_SO or u < U_AO:
                        return
                    dve.wait_ge(chunk_done, unit_end(l, u))
                    if u < U_GM:
                        g = gates[:, 0, j:j + 2, :].rearrange("p k t -> p (k t)")
                        stt(g, g, 1.0, gemm[u % 2][:], ALU.add, ALU.mult).then_inc(gemm_read[u % 2], 1)
                    else:
                        ssm_output(u)

                def ssm_output(u):
                    b, j = u % 2, 2 * (u % 4)
                    dve.drain()
                    stt(gated[:, b, :], gates[:, 1, j:j + 2, :].rearrange("p k t -> p (k t)"), 1.0, gemm[b][:],
                        ALU.add, ALU.mult).then_inc(gemm_read[b], 1)
                    dve.drain()
                    mx = gates[:, 0, j:j + 2, :].rearrange("p k t -> p (k t)")
                    return V.tensor_tensor(mx, gated[:, b, :], mx, ALU.add)

                def y_gate(f):
                    b, k = O.use(l, O_Y + f)
                    dve.wait_ge(y_done, l * 32 + 2 * f + 2)
                    if f:
                        mods(ada_scan(l, f - 1), 1, O.bank[b][:, SEQ:SEQ + 1])
                    stt(work[:, f % 2, 0:SEQ], xs[:, f, :], col("skip", f), O.bank[b][:, 0:SEQ], ALU.mult, ALU.add
                        ).then_inc(O.read[b], 1)
                    dve.drain()
                    if f == 0:
                        dve.wait_ge(z_ready, 8 * (l + 1))
                    V.tensor_tensor(zg[:, f, :], work[:, f % 2, 0:SEQ], zg[:, f, :], ALU.mult).then_inc(y_gated, 1)

                for g in range(SSM_GROUPS):
                    b, k = S.use(l, S_CB + g)
                    dve.wait_ge(S.full[b], k + 1)
                    if g == 1:
                        mods(ada_attention(l, HEADS - 2), 2, S.bank[b][:, CW:CW + 2])
                    V.tensor_copy(CB[:, g, :], S.bank[b][:, 0:CW]).then_inc(S.read[b], 1)
                turn_o(l, T_OT)
                dve.drain().then_inc(oT_ready, 1)
                for hf in range(2):
                    before, at_head, after = SCAN_CHUNKS[hf]
                    for c in before:
                        scan_chunk(c)
                    tx, ts = t_half(hf)
                    if hf:
                        dve.wait_ge(y_done, l * 32 + 16)
                    for r in range(4):
                        b, k = T.use(l, tx + r)
                        dve.wait_ge(T.full[b], k + 1)
                        h0 = 16 * hf + 4 * r
                        for tt in range(TT):
                            ins = V.tensor_tensor(xdt[:, tt, 256 * r:256 * r + 256].rearrange("p (h d) -> p h d", d=HD),
                                                  T.bank[b][:, 256 * tt:256 * tt + 256].rearrange("p (h d) -> p h d", d=HD),
                                                  dt_s[:, tt, h0:h0 + 4].unsqueeze(2).to_broadcast([P, 4, HD]), ALU.mult)
                        ins.then_inc(T.read[b], 1)
                    dve.drain()
                    for h in range(16 * hf, 16 * hf + 16):
                        b, k = S.use(l, S_SSM + h)
                        n = l * 32 + h
                        dve.wait_ge(S.read[b], k + 1)
                        if n >= 2:
                            dve.wait_ge(y_done, n - 1)
                        V.tensor_tensor(probsT[:, h % 2, :], probs[:, b, :], CB[:, h // 8, :], ALU.mult).then_inc(g_ready, 1)
                        if h % 2 and h > 16 * hf + 1:
                            y_gate(h // 2 - 1)
                        if h % 16:
                            for c in at_head[h % 16 - 1]:
                                scan_chunk(c)
                        if h % 2 == 0:
                            ada(ada_scan(l, h // 2))
                    for c in at_head[15]:
                        scan_chunk(c)
                    y_gate(8 * hf + 7)
                    for c in after:
                        scan_chunk(c)
                    for gi in range(2):
                        b, k = T.use(l, ts + gi)
                        dve.wait_ge(T.full[b], k + 1)
                        V.tensor_scalar(work[:, gi, 0:SEQ], T.bank[b][:, 0:SEQ], 1.0 / 512, EPS, ALU.mult, ALU.add
                                        ).then_inc(T.read[b], 1)
                    dve.wait_ge(y_root, 4 * l + 2 * hf + 2)
                    dve.drain()
                    rsqrt(rs[:, 0:2, :], work[:, 0:2, 0:SEQ], work[:, 2:4, 0:SEQ])
                    for f in range(8):
                        t = 8 * hf + f
                        stt(zg[:, t, :], zg[:, t, :], col("ssmn", t), rs[:, f // 4, :], ALU.mult, ALU.mult).then_inc(y_scaled, 1)
                    for f in range(8):
                        n = l * 16 + 8 * hf + f
                        dve.wait_ge(y_hi, n + 1)
                        V.tensor_tensor(OTL[:, f, :], zg[:, 8 * hf + f, :], OTH[:, f, :].bitcast(f32), ALU.subtract
                                        ).then_inc(y_ready, 1)
                for u in range(U_SO + 4, U_SO + 8):
                    dve.wait_ge(chunk_done, unit_end(l, u))
                    ssm_output(u).then_inc(mix_ready, 1)
                for j in range(4):
                    dve.wait_ge(mix_hi, l * 4 + j + 1)
                    stt(HL[:, 2 * j:2 * j + 2, :], gates[:, 0, 2 * j:2 * j + 2, :], 0.5,
                        HH[:, 2 * j:2 * j + 2, :].bitcast(f32), ALU.mult, ALU.subtract).then_inc(mix_low, 1)
                for j in range(4):
                    dve.wait_ge(chunk_done, unit_end(l, U_OUT + j))
                    add_to_x(l, U_OUT + j, j, mod[:, l, 16:24])
                norm(l, 1, col("norm2", 0, KT), mod[:, l, 32:40], mod[:, l, 24:32])
                def up_product(i):
                    dve.wait_ge(up_silu, l * FT + i + 1)
                    dve.drain()
                    w = work[:, i % 4, 0:SEQ]
                    V.tensor_tensor(w, w, conv[:, i % 2, 0:SEQ], ALU.mult).then_inc(up_prod, 1)

                def up_low(i):
                    dve.wait_ge(up_hi, l * FT + i + 1)
                    V.tensor_tensor(FL[:, i, :], work[:, i % 4, 0:SEQ], FH[:, i, :].bitcast(f32), ALU.subtract).then_inc(up_ready, 1)

                for u in range(U_UP, U_DN):
                    i = u - U_UP
                    b, k = gemm_use(l, u)
                    dve.wait_ge(up_first, l * FT + i + 1)
                    for d in range(1, FFN_CONV):
                        if d > 1:
                            dve.drain()
                        for j in range(2):
                            o = j * SEQ
                            c = conv[:, i % 2, o + d:o + SEQ]
                            ins = stt(c, gemm[b][:, o:o + SEQ - d], col("ffnw", (2 - d) * 2 * FT + j * FT + i), c, ALU.mult, ALU.add)
                    ins.then_inc(gemm_read[b], 1)
                    if i >= 1:
                        up_product(i - 1)
                    if i >= 2:
                        up_low(i - 2)
                up_product(FT - 1)
                up_low(FT - 2)
                up_low(FT - 1)
                dve.drain()
                for j in range(4):
                    if l + 1 < DEPTH:
                        for i in range(4 * j, 4 * j + 4):
                            ada(ada_down(l, i))
                    dve.wait_ge(chunk_done, l * NCH + 2 * U_DN + (j + 1) * DN_CHUNKS)
                    add_to_x(l, U_DN + j, j, mod[:, l, 40:48])
                if l + 1 < DEPTH:
                    dve.wait_ge(ada_summed, ada_down(l, 0))
                    mods(ada_down(l, 0), 2 * KT, mod_ps)
                dve.drain()

            l = DEPTH
            norm(l, 0, prm2[:, 0:KT], None, None)
            dve.wait_ge(tab_full, 32)
            for i in range(2):
                for b in range(2):
                    k = gemm_use(l, 4 * i + 2 + b)[1]
                    dve.wait_ge(gemm_read[b], k + 1)
                qk_norm(l, i, None)
                dve.drain()
                x = qkv[:, i]
                V.tensor_tensor(x, x, bc3(rows2_sb[:, i, :], D, TT), ALU.mult)
                dve.drain().then_inc(qk_rot, 1)
            b, k = gemm_use(l, V_G)
            dve.wait_ge(gemm_read[b], k + 1)
            n_f = TT * N_FOX
            nf = small[:, 226:226 + n_f]
            V.tensor_tensor(nf.rearrange("p (t h) -> p t h", t=TT), g2[:, :, 0:N_FOX], bc3(prm2[:, 2 * KT:], N_FOX, TT), ALU.add)
            dve.drain()
            stt(small[:, 0:n_f], nf, -1.0, nf, ALU.mult, ALU.min)
            V.tensor_scalar(small[:, 240:240 + n_f], nf, -1.0, None, ALU.mult)
            dve.drain().then_inc(sp_in, 1)
            dve.wait_ge(sp_exp, 2 * l + 1)
            softplus(small[:, 240:240 + n_f], small[:, 0:n_f], n_f, -1)
            dve.drain().then_inc(a_ready, 1)
            b, k = T.use(l, T2_A)
            dve.wait_ge(T.full[b], k + 1)
            V.tensor_copy(a_row[0:N_FOX, :], T.bank[b][0:N_FOX, 0:SEQ]).then_inc(T.read[b], 1)
            dve.drain()
            V.tensor_tensor_scan(out=cs_row[0:N_FOX, :], data0=ones[0:N_FOX, :], data1=a_row[0:N_FOX, :], initial=0.0,
                                 op0=ALU.mult, op1=ALU.add).then_inc(cs_ready, 1)
            for i in range(N_FOX):
                b, k = S.use(l, S2_FOX + i)
                dve.wait_ge(S.full[b], k + 1)
                stt(fox_bias[:, i, 0:P], S.bank[b][:, 0:P], -1.0 / SCALE, causal[:, 0:P], ALU.mult, ALU.add)
                stt(fox_bias[:, i, P:CW], S.bank[b][:, 0:SEQ], -1.0 / SCALE, causal[:, P:CW], ALU.mult, ALU.add
                    ).then_inc(S.read[b], 1)
            turn_qk(l, T2_QK)
            fox_end = N_MOBA + N_FOX

            def bias2(h):
                if h < N_MOBA:
                    return alibi_sb[:, h, :]
                if h < fox_end:
                    return fox_bias[:, h - N_MOBA, :]
                return alibi_sb[:, h - N_FOX, :]

            attention(l, bias2)
            spans = ((0, N_MOBA * HD), (N_MOBA * HD, fox_end * HD), (fox_end * HD, D))
            for tt in range(TT):
                for i, (a, e) in enumerate(spans):
                    w = work[:, i, 0:e - a]
                    dve.drain()
                    V.tensor_tensor(w, o_tok[:, tt, a:e], o_tok[:, tt, a:e], ALU.mult)
                    dve.drain()
                    V.tensor_reduce(out=small[:, 3 * tt + i:3 * tt + i + 1], in_=w, axis=AX.X, op=ALU.add)
            dve.drain()
            for tt in range(TT):
                for i, (a, e) in enumerate(spans):
                    r = small[:, 3 * tt + i:3 * tt + i + 1]
                    V.tensor_scalar(r, r, 1.0 / (e - a), EPS, ALU.mult, ALU.add)
            dve.drain().then_inc(og_in, 1)
            dve.wait_ge(og_root, 1)
            rsqrt(root[:, 2, 0:6], small[:, 0:6], work[:, 0, 0:6])
            for tt in range(TT):
                for i, (a, e) in enumerate(spans):
                    stt(o_tok[:, tt, a:e], o_tok[:, tt, a:e], root[:, 2, 3 * tt + i:3 * tt + i + 1], rows2_sb[:, 2, a:e],
                        ALU.mult, ALU.mult)
            dve.drain()
            a, e = spans[1]
            V.tensor_tensor(o_tok[:, :, a:e], o_tok[:, :, a:e], g2[:, :, N_FOX:], ALU.mult)
            dve.drain().then_inc(o_ready, 1)
            turn_o(l, T2_OT)
            dve.drain().then_inc(oT_ready, 1)
            for j in range(4):
                dve.wait_ge(chunk_done, unit_end(l, V_OUT + j))
                add_to_x(l, V_OUT + j, j, None)
            norm(l, 1, prm2[:, KT:2 * KT], None, None)

            def up2_low(i):
                dve.wait_ge(up_hi, DEPTH * FT + i + 1)
                V.tensor_tensor(F2L[:, 2 * i:2 * i + 2, :].rearrange("p k t -> p (k t)"), work[:, i % 4, :],
                                F2H[:, 2 * i:2 * i + 2, :].rearrange("p k t -> p (k t)").bitcast(f32), ALU.subtract
                                ).then_inc(up_ready, 1)

            for u in range(V_UP, V_DN):
                i = u - V_UP
                b, k = gemm_use(l, u)
                dve.wait_ge(up_first, DEPTH * FT + i + 1)
                if i >= 4:
                    dve.drain()
                stt(work[:, i % 4, :], gemm[b][:], 0.0, conv[:, i % 2, :], ALU.max, ALU.mult).then_inc(gemm_read[b], 1)
                if i >= 1:
                    up2_low(i - 1)
            up2_low(V_DN - V_UP - 1)
            for j in range(4):
                dve.wait_ge(chunk_done, DEPTH * NCH + 2 * V_DN + (j + 1) * DN2_CHUNKS)
                add_to_x(l, V_DN + j, j, None)

        @block.tensor
        def _(pe):
            M = nc.tensor.matmul

            def products(passes, first, last):
                for i, (o, a, b) in enumerate(passes):
                    ins = M(o, a, b, start=first and i == 0, stop=last and i == len(passes) - 1, skip_group_check=True)
                return ins

            def weights(g):
                pe.wait_ge(hi_ready, g + 1)
                pe.wait_ge(lo_ready, g + 1)
                l = min(g // NCH, DEPTH)
                return g % RING, chunk_words(l, g - l * NCH)

            def feature_chunk(g, out, xh, xl, k0, first, last):
                s, n = weights(g)
                kts = n // 256
                wh = w_hi[:, s, 0:n].rearrange("p (k n) -> p k n", n=256)
                wl = w_lo[:, s, 0:n].rearrange("p (k n) -> p k n", n=256)
                passes = []
                for j in range(2):
                    o = out[:, j * SEQ:(j + 1) * SEQ]
                    c = slice(j * P, (j + 1) * P)
                    for k in range(kts):
                        passes += [(o, wh[:, k, c], xh[:, k0 + k, :]), (o, wh[:, k, c], xl[:, k0 + k, :]),
                                   (o, wl[:, k, c], xh[:, k0 + k, :])]
                products(passes, first, last).then_inc(chunk_done, 1)

            def token_chunk(g, out, xh, xl, k0, first, last):
                s, n = weights(g)
                w = n // 4
                wh = w_hi[:, s, 0:n].rearrange("p (k n) -> p k n", k=4)
                wl = w_lo[:, s, 0:n].rearrange("p (k n) -> p k n", k=4)
                passes = []
                for j in range(TT):
                    o = out[:, j * 256:j * 256 + w]
                    c = slice(j * P, (j + 1) * P)
                    for k in range(4):
                        passes += [(o, xh[:, k0 + k, c], wh[:, k, :]), (o, xh[:, k0 + k, c], wl[:, k, :]),
                                   (o, xl[:, k0 + k, c], wh[:, k, :])]
                products(passes, first, last).then_inc(chunk_done, 1)

            def free_gemm(l, o):
                b, k = gemm_use(l, o)
                if k:
                    pe.wait_ge(gemm_read[b], k)
                return gemm[b]

            def half_unit(l, u, second, chunk, xh, xl):
                out = gemm[u % 2] if second else free_gemm(l, u)
                chunk(first_chunk(l, u) + second, out, xh, xl, 4 * second, not second, bool(second))

            def unit(l, u, chunk, xh, xl, h_count=None):
                half_unit(l, u, 0, chunk, xh, xl)
                if h_count is not None:
                    pe.wait_ge(h_ready, h_count)
                half_unit(l, u, 1, chunk, xh, xl)

            def take(pair, l, i):
                b, k = pair.use(l, i)
                if k:
                    pe.wait_ge(pair.read[b], k)
                return b, pair.bank[b]

            def arrived(pair, l, i):
                b, k = pair.use(l, i)
                pe.wait_ge(pair.read[b], k + 1)

            def ada_tile(a, out):
                pe.wait_ge(ada_full[a % 2], 16 * (a // 2 + 1))
                for k in range(KT):
                    ins = M(out, ada_w[:, a % 2, k * P:(k + 1) * P], c_act[:, k:k + 1], start=k == 0, stop=k == KT - 1)
                ins.then_inc(ada_used, 1)

            def ada_sum(a, out):
                pe.wait_ge(ada_used, a + 1)
                M(out, ada_acc[:, a % 4, :], ones[:, 0:1], start=True, stop=True).then_inc(ada_summed, 1)

            def norm_sum(l, which):
                i = (O_N2 if which else O_N1) if l < DEPTH else (O2_N2 if which else O2_N1)
                b, out = take(O, l, i)
                if l < DEPTH and which:
                    ada_sum(ada_scan(l, 15), out[:, SEQ:SEQ + 1])
                for kt in range(KT):
                    if kt % 2 == 0:
                        pe.wait_ge(sq_ready, (2 * l + which) * 4 + kt // 2 + 1)
                    ins = M(out[:, 0:SEQ], ones[:, 0:P], sq[:, kt, :], start=kt == 0, stop=kt == KT - 1)
                ins.then_inc(o_full, 1)
                pe.wait_ge(h_ready, (2 * l + which) * KT + KT // 2)
                return (2 * l + which + 1) * KT

            def turn(l, i, blocks):
                b, out = take(T, l, i)
                for c, rows, src, n in blocks:
                    ins = nc.tensor.transpose(out[0:rows, c:c + n], src, ident[0:n, 0:n])
                ins.then_inc(T.full[b], 1)

            def turn_tokens(l, t0, src_of, rounds):
                for r in range(rounds):
                    src = src_of(r)
                    turn(l, t0 + r, [(j * SEQ + tt * P, P, src[:, tt, j * P:(j + 1) * P], P)
                                     for j in range(2) for tt in range(TT)])

            def attention(l):
                s0, t0, o0 = (S_AT, T_AT, O_AT) if l < DEPTH else (S2_AT, T2_AT, O2_AT)

                def scores(h):
                    b, out = take(S, l, s0 + h)
                    if l < DEPTH and h % 2 and h > 1:
                        for i in range(2):
                            ada_sum(ada_attention(l, h - 3) + i, out[:, CW + i:CW + i + 1])
                    r = slice(64 * (h % 2), 64 * (h % 2) + 64)
                    M(out[:, 0:P], qT[r, h // 2, 0:P], kT[r, h // 2, 0:P], start=True, stop=True)
                    M(out[:, P:CW], qT[r, h // 2, P:SEQ], kT[r, h // 2, :], start=True, stop=True).then_inc(S.full[b], 1)

                def values(h):
                    arrived(T, l, t0 + h)
                    i = o0 + h // 4
                    b, k = O.use(l, i)
                    if h % 4 == 0:
                        take(O, l, i)
                    c = (h % 4) * P
                    v = qkv[:, 2, :, h * HD:(h + 1) * HD]
                    pT = probsT[:, h % 2, :]
                    M(O.bank[b][:, c:c + HD], pT[:, 0:P], v[:, 0, :], start=True, stop=True)
                    M(O.bank[b][:, c + HD:c + P], pT[:, P:2 * P], v[:, 0, :], start=True, stop=False)
                    ins = M(O.bank[b][:, c + HD:c + P], pT[:, 2 * P:CW], v[:, 1, :], start=False, stop=True)
                    if h % 4 == 3:
                        ins.then_inc(o_full, 1)

                scores(0)
                for h in range(HEADS):
                    if h + 1 < HEADS:
                        scores(h + 1)
                    if l < DEPTH:
                        half_unit(l, U_Z + h // 2, h % 2, feature_chunk, HH, HL)
                    pe.wait_ge(exp_done, l * HEADS + h + 1)
                    turn(l, t0 + h, [(c, P, probs[:, h % 2, c:c + P], P) for c in (0, P, 2 * P)])
                    if h:
                        values(h - 1)
                values(HEADS - 1)

            pe.wait_ge(set_up, 1)
            pe.wait_ge(c_silu, 1)
            for a in range(2 * KT):
                ada_tile(a, mod_ps[:, a:a + 1])
            for l in range(DEPTH):
                h_count = norm_sum(l, 0)
                for u in range(U_IDX, U_Q + 2):
                    unit(l, u, token_chunk, HH, HL, h_count if u == U_IDX else None)
                pe.wait_ge(idx_rot, l + 1)
                turn_tokens(l, T_IQ, lambda r: iq[:, :, 256 * r:256 * r + 256], 2)
                turn(l, T_IQ + 2, [(tt * P, P, ik[:, tt, :], P) for tt in range(TT)])
                for r in range(3):
                    arrived(T, l, T_IQ + r)
                for h in range(IDX_HEADS):
                    b, o = take(S, l, S_IDX + h)
                    r = slice(64 * (h % 2), 64 * (h % 2) + 64)
                    M(o[:, 0:P], iqT[r, h // 2, 0:P], ikT[r, 0:P], start=True, stop=True)
                    M(o[:, P:CW], iqT[r, h // 2, P:SEQ], ikT[r, :], start=True, stop=True).then_inc(S.full[b], 1)
                pe.wait_ge(a_ready, l + 1)
                turn(l, T_A, [(tt * P, 32, small[:, 32 * tt:32 * tt + 32], P) for tt in range(TT)])
                for u in range(U_Q + 2, U_XBC):
                    unit(l, u, token_chunk, HH, HL)
                pe.wait_ge(cs_ready, l + 1)
                b, o = take(T, l, T_CS)
                for tt in range(TT):
                    ins = nc.tensor.transpose(o[:, 32 * tt:32 * tt + 32], cs_row[0:32, tt * P:(tt + 1) * P], ident[0:32, 0:32])
                ins.then_inc(T.full[b], 1)
                for u in range(U_XBC, U_Z):
                    unit(l, u, feature_chunk, HH, HL)
                pe.wait_ge(qk_rot, 2 * l + 2)
                turn_tokens(l, T_QK, lambda r: qkv[:, r // 4, :, 256 * (r % 4):256 * (r % 4) + 256], 8)
                for r in range(6, 8):
                    arrived(T, l, T_QK + r)
                attention(l)
                pe.wait_ge(conv_act, (l + 1) * 12)
                for g in range(SSM_GROUPS):
                    b, o = take(S, l, S_CB + g)
                    if g == 1:
                        for i in range(2):
                            ada_sum(ada_attention(l, HEADS - 2) + i, o[:, CW + i:CW + i + 1])
                    M(o[:, 0:SEQ], bc[:, g, 0:P], bc[:, SSM_GROUPS + g, :], start=True, stop=True)
                    M(o[:, SEQ:CW], bc[:, g, P:SEQ], bc[:, SSM_GROUPS + g, P:SEQ], start=True, stop=True).then_inc(S.full[b], 1)
                pe.wait_ge(o_ready, l + 1)
                turn_tokens(l, T_OT, lambda r: o_tok[:, :, 256 * r:256 * r + 256], 4)

                def scan_chunk(c):
                    u, second = scan_unit(c)
                    if u == U_AO and not second:
                        pe.wait_ge(oT_ready, l + 1)
                    if u == U_SO and not second:
                        pe.wait_ge(y_ready, l * 16 + 8)
                    x = (OTH, OTL) if U_AO <= u < U_GM or u >= U_SO else (HH, HL)
                    half_unit(l, u, second, feature_chunk, *x)

                def decay_exponents(h):
                    b, o = take(S, l, S_SSM + h)
                    pick = ident[:, h:h + 1].to_broadcast([P, P])
                    ins = products([(o[:, 0:SEQ], pick, cs_row[:, :]), (o[:, SEQ:CW], pick, cs_row[:, P:SEQ]),
                                    (o[:, 0:P], ident_b[:], maskT_b[:]), (o[:, SEQ:CW], ident_b[:], maskT_b[:])], True, True)
                    ins.then_inc(S.full[b], 1)

                def head_y(h):
                    pe.wait_ge(g_ready, l * 32 + h + 1)
                    b, k = O.use(l, O_Y + h // 2)
                    if h % 2 == 0:
                        take(O, l, O_Y + h // 2)
                    r = slice(64 * (h % 2), 64 * (h % 2) + 64)
                    c = (h % 16) * HD
                    M(O.bank[b][r, 0:SEQ], xdt[:, 0, c:c + HD], probsT[:, h % 2, 0:SEQ], start=True, stop=False)
                    M(O.bank[b][r, P:SEQ], xdt[:, 1, c:c + HD], probsT[:, h % 2, SEQ:CW], start=False, stop=True).then_inc(y_done, 1)
                    if h % 2 == 0 and h:
                        ada_sum(ada_scan(l, h // 2 - 1), O.bank[b][:, SEQ:SEQ + 1])

                for hf in range(2):
                    tx, ts = t_half(hf)
                    before, at_head, after = SCAN_CHUNKS[hf]
                    for c in before:
                        scan_chunk(c)
                    for r in range(4):
                        turn(l, tx + r, [(tt * SEQ + j * P, P, xs[:, 8 * hf + 2 * r + j, tt * P:(tt + 1) * P], P)
                                         for tt in range(TT) for j in range(2)])

                    def square_sum(f):
                        b, k = T.use(l, ts + (f % 8) // 4)
                        if f % 4 == 0:
                            take(T, l, ts + (f % 8) // 4)
                        pe.wait_ge(y_sq, l * 16 + f + 1)
                        ins = M(T.bank[b][:, 0:SEQ], ones[:, 0:P], work[:, f % 4, SEQ:2 * SEQ], start=f % 4 == 0, stop=f % 4 == 3)
                        if f % 4 == 3:
                            ins.then_inc(T.full[b], 1)

                    h0 = 16 * hf
                    decay_exponents(h0)
                    for r in range(2, 4):
                        arrived(T, l, tx + r)
                    for h in range(h0, h0 + 16):
                        if h + 1 < h0 + 16:
                            decay_exponents(h + 1)
                        for c in at_head[h % 16]:
                            scan_chunk(c)
                        head_y(h)
                        if h % 2 == 0 and h >= h0 + 4:
                            square_sum(h // 2 - 2)
                    square_sum(8 * hf + 6)
                    square_sum(8 * hf + 7)
                    for c in after:
                        scan_chunk(c)
                pe.wait_ge(y_ready, (l + 1) * 16)
                for u in range(U_SO + 4, U_SO + 8):
                    unit(l, u, feature_chunk, OTH, OTL)
                pe.wait_ge(mix_low, 4 * (l + 1))
                for u in range(U_OUT, U_UP):
                    unit(l, u, feature_chunk, HH, HL)
                h_count = norm_sum(l, 1)
                for u in range(U_UP, U_DN):
                    unit(l, u, feature_chunk, HH, HL, h_count if u == U_UP else None)
                for j in range(4):
                    out_b = free_gemm(l, U_DN + j)
                    for c in range(DN_CHUNKS):
                        if j == 0:
                            pe.wait_ge(up_ready, l * FT + min(4 * c + 4, FT))
                        feature_chunk(l * NCH + 2 * U_DN + j * DN_CHUNKS + c, out_b, FH, FL, 4 * c, c == 0, c == DN_CHUNKS - 1)
                        if l + 1 < DEPTH and 1 <= c < 5:
                            i = 4 * j + c - 1
                            ada_sum(ada_down(l, i), mod_ps[:, i:i + 1])

            l = DEPTH
            h_count = norm_sum(l, 0)
            for u in range(0, V_OUT):
                unit(l, u, token_chunk, HH, HL, None if u else h_count)
            pe.wait_ge(a_ready, l + 1)
            turn(l, T2_A, [(tt * P, N_FOX, small[:, 240 + N_FOX * tt:240 + N_FOX * (tt + 1)], P) for tt in range(TT)])
            pe.wait_ge(qk_rot, 2 * l + 2)
            pe.wait_ge(cs_ready, l + 1)
            for i in range(N_FOX):
                b, o = take(S, l, S2_FOX + i)
                M(o[:, 0:SEQ], ident[:, i:i + 1].to_broadcast([P, P]), cs_row[:, :], start=True, stop=True).then_inc(S.full[b], 1)
            turn_tokens(l, T2_QK, lambda r: qkv[:, r // 4, :, 256 * (r % 4):256 * (r % 4) + 256], 8)
            for r in range(6, 8):
                arrived(T, l, T2_QK + r)
            attention(l)
            pe.wait_ge(o_ready, l + 1)
            turn_tokens(l, T2_OT, lambda r: o_tok[:, :, 256 * r:256 * r + 256], 4)
            pe.wait_ge(oT_ready, l + 1)
            for u in range(V_OUT, V_UP):
                unit(l, u, feature_chunk, OTH, OTL)
            h_count = norm_sum(l, 1)
            for u in range(V_UP, V_DN):
                unit(l, u, feature_chunk, HH, HL, h_count if u == V_UP else None)
            for j in range(4):
                out_b = free_gemm(l, V_DN + j)
                for c in range(DN2_CHUNKS):
                    if j == 0:
                        pe.wait_ge(up_ready, DEPTH * FT + 2 * c + 2)
                    feature_chunk(l * NCH + 2 * V_DN + j * DN2_CHUNKS + c, out_b, F2H, F2L, 4 * c, c == 0, c == DN2_CHUNKS - 1)


def shape_constants():
    t, s = np.arange(SEQ)[:, None], np.arange(SEQ)[None, :]

    def blocks(a):
        return np.concatenate([a[0:P, 0:P], a[P:SEQ, 0:SEQ]], axis=1)

    causal = np.where(s <= t, 0.0, NEG)
    inv = np.float32(1.0) / (10000.0 ** (np.arange(0, HD, 2) / HD)).astype(np.float32)
    consts = np.concatenate([np.eye(P), blocks(causal), causal[0:P, 0:P].T, np.tile(inv[None], (P, 1))], axis=1)
    n_alibi = N_MOBA + N_DIL
    slopes = 2.0 ** (-8.0 * np.arange(1, n_alibi + 1) / n_alibi)
    dist = t - s
    seen = (dist <= 128) * 1.0 + (dist % 4 == 0) + (dist % 16 == 0)
    alibi = []
    for h in range(N_MOBA):
        alibi.append(blocks(np.where(s <= t, -slopes[N_DIL + h] * dist / SCALE, NEG)))
    for h in range(N_DIL):
        alibi.append(blocks(np.where((s <= t) & (seen > 0), (np.log(np.maximum(seen, 1.0)) - slopes[h] * dist) / SCALE, NEG)))
    return consts.astype(np.float32), np.stack(alibi, axis=1).astype(np.float32)


def stream_of(w_in, w_attn_o, w_ssm_o, w_out, w_up, w_down, w_in_2, w_out_2, w_up_2, w_down_2):
    parts = []

    def chunk(w, row_tile, kts, c0, width):
        a = w[row_tile * P:(row_tile + kts) * P, c0:c0 + width]
        parts.append(a.reshape(kts, P, width).transpose(1, 0, 2).reshape(-1))

    def unit(w, c0, width=256, row_tile=0):
        chunk(w, row_tile, 4, c0, width)
        chunk(w, row_tile + 4, 4, c0, width)

    q, k, v, iq, ik, iw, z, xbc, dt, ga, gm, end = np.cumsum(
        [0, D, D, D, IDX_HEADS * HD, HD, IDX_HEADS, D_INNER, XBC_TILES * P, SSM_HEADS, D, D]).tolist()
    for l in range(DEPTH):
        w = w_in[l]
        for c in (iq, iq + 256):
            unit(w, c)
        unit(w, ik, HD + IDX_HEADS)
        unit(w, dt, SSM_HEADS)
        for a, e in ((q, iq), (xbc, dt), (z, xbc), (ga, gm)):
            for c in range(a, e, 256):
                unit(w, c)
        for c in range(0, D, 256):
            unit(w_attn_o[l], c)
        for c in range(gm, end, 256):
            unit(w, c)
        for hf in range(2):
            for c in range(0, D, 256):
                unit(w_ssm_o[l], c, 256, KT * hf)
        for c in range(0, D, 256):
            unit(w_out[l], c)
        up = w_up[l].reshape(D, 2, FT, P).transpose(0, 2, 1, 3).reshape(D, 2 * D_FF)
        for i in range(FT):
            unit(up, 256 * i)
        for c in range(0, D, 256):
            for i in range(DN_CHUNKS):
                chunk(w_down[l], 4 * i, min(4, FT - 4 * i), c, 256)
    w = w_in_2[0]
    for c in range(0, 3 * D, 256):
        unit(w, c)
    unit(w, 3 * D)
    unit(w, 3 * D + 256, G_COLS - 256)
    for c in range(0, D, 256):
        unit(w_out_2[0], c)
    for c in range(0, D_FF2, 256):
        unit(w_up_2[0], c)
    for c in range(0, D, 256):
        for i in range(DN2_CHUNKS):
            chunk(w_down_2[0], 4 * i, 4, c, 256)
    return np.concatenate(parts)


def kernel(x, c, positions, w_ada, b_ada, norm1_g, w_in, q_norm_g, k_norm_g, ssm_conv_w, ssm_conv_b, dt_bias, a_log,
           d_skip, ssm_norm_g, w_attn_o, w_ssm_o, w_out, norm2_g, w_up, ffn_conv_w, ffn_conv_b, w_down, attn_norm_2,
           w_in_2, b_forget_2, q_gain_2, k_gain_2, out_gain_2, w_out_2, mlp_norm_2, w_up_2, w_down_2):
    import concourse.bacc as bacc
    from concourse.bass_utils import run_bass_kernel_spmd

    def tiles(a):
        return np.asarray(a).reshape(-1, P).T

    def rows(a):
        return np.tile(np.asarray(a).reshape(1, -1), (P, 1))

    consts, alibi = shape_constants()
    params = np.stack([np.concatenate([
        tiles(norm1_g[l]), tiles(norm2_g[l]), tiles(ssm_norm_g[l]), tiles(ssm_conv_b[l]), tiles(ssm_conv_w[l]),
        tiles(ffn_conv_b[l]), tiles(ffn_conv_w[l]), tiles(np.repeat(np.asarray(d_skip[l]), HD)), rows(dt_bias[l]),
        rows(a_log[l]), rows(q_norm_g[l]), rows(k_norm_g[l])], axis=1) for l in range(DEPTH)])
    ada = np.stack([np.asarray(w_ada[l]).reshape(KT, P, 48, P).transpose(2, 1, 0, 3).reshape(48, P, KT * P)
                    for l in range(DEPTH)]).reshape(DEPTH * 48, P, KT * P)
    arrays = {
        "x_t": np.asarray(x)[0].T,
        "c_col": tiles(c),
        "pos": np.asarray(positions).reshape(TT, P).T,
        "consts": consts,
        "alibi": alibi,
        "params": params,
        "b_ada": np.concatenate([tiles(b_ada[l]) for l in range(DEPTH)], axis=1),
        "params2": np.concatenate([tiles(attn_norm_2[0]), tiles(mlp_norm_2[0]), rows(b_forget_2[0])], axis=1),
        "rows2": np.stack([rows(q_gain_2[0]), rows(k_gain_2[0]), rows(out_gain_2[0])], axis=1),
        "w_ada": ada,
        "stream": stream_of(*(np.asarray(a) for a in (w_in, w_attn_o, w_ssm_o, w_out, w_up, w_down,
                                                      w_in_2, w_out_2, w_up_2, w_down_2))),
    }
    nc = bacc.Bacc("TRN2", target_bir_lowering=False, num_devices=1)
    args, ins = [], {}
    for name, a in arrays.items():
        ins[f"in_{name}"] = np.ascontiguousarray(a)
        args.append(nc.dram_tensor(f"in_{name}", a.shape, mybir.dt.from_np(a.dtype), kind="ExternalInput").ap())
    out = nc.dram_tensor("out_x", (D, SEQ), mybir.dt.float32, kind="ExternalOutput").ap()
    build(nc, *args, out)
    r = run_bass_kernel_spmd(nc, [ins], core_ids=[0])
    return np.ascontiguousarray(r.results[0]["out_x"].T)[None]
```
